# Optimizing a Trainium2 kernel written in Bass

```python
import jax, jax.numpy as jnp
from jax import lax
import numpy as np

D_MODEL = 1024
BATCH = 1
SEQ = 256
DEPTH = 2

N_A_LAYERS = DEPTH // 2
N_B_LAYERS = DEPTH - N_A_LAYERS
N_DENSE = (DEPTH + 1) // 2
N_MOE = DEPTH // 2

D_RNN = D_MODEL
RNN_BLOCKS = 8
RNN_BLOCK_W = D_RNN // RNN_BLOCKS
CONV_W = 4
LRU_C = 8.0

HEAD_DIM = 64
N_Q_HEADS = D_MODEL // HEAD_DIM
N_KV_HEADS = 4
GROUP = N_Q_HEADS // N_KV_HEADS
WINDOW = 128
BLOCK = 128
ROPE_THETA = 10000.0

D_FF = 3 * D_MODEL
N_EXPERTS = 8
TOP_K = 2
D_FF_EXPERT = 7 * D_MODEL // 2

EPS = 1e-6
F32 = jnp.float32

kernel_name = "hybrid_rglru_yoco_swa_sink_moe"

def rms_norm(x, g):
    x32 = x.astype(F32)
    y = x32 * lax.rsqrt(jnp.mean(x32 * x32, axis=-1, keepdims=True) + EPS)
    return (y * g.astype(F32)).astype(x.dtype)

def modulate(x, g, shift, scale):
    return rms_norm(x, g) * (1 + scale[:, None, :]) + shift[:, None, :]

def rope_tables(positions, dtype):
    inv = ROPE_THETA ** (-jnp.arange(0, HEAD_DIM, 2, dtype=F32) / HEAD_DIM)
    ang = positions.astype(F32)[..., None] * inv
    return jnp.cos(ang)[:, :, None, :].astype(dtype), jnp.sin(ang)[:, :, None, :].astype(dtype)

def rotary(x, cos, sin):
    x1, x2 = jnp.split(x, 2, axis=-1)
    return jnp.concatenate([x1 * cos - x2 * sin, x2 * cos + x1 * sin], axis=-1)

def rglru_mixer(h, w_in, conv_w, conv_b, gx_w, gx_b, ga_w, ga_b, lam, w_out):
    bsz, seq, _ = h.shape
    xb, yb = jnp.split(h @ w_in, 2, axis=-1)
    xp = jnp.pad(xb, ((0, 0), (CONV_W - 1, 0), (0, 0)))
    xc = conv_b + xp[:, 0:seq] * conv_w[0]
    for k in range(1, CONV_W):
        xc = xc + xp[:, k:k + seq] * conv_w[k]
    xblk = xc.reshape(bsz, seq, RNN_BLOCKS, RNN_BLOCK_W)
    r_gate = jax.nn.sigmoid((jnp.einsum('bsnc,ncd->bsnd', xblk, ga_w).reshape(bsz, seq, D_RNN) + ga_b).astype(F32))
    i_gate = jax.nn.sigmoid((jnp.einsum('bsnc,ncd->bsnd', xblk, gx_w).reshape(bsz, seq, D_RNN) + gx_b).astype(F32))
    log_a = -LRU_C * r_gate * jax.nn.softplus(-lam.astype(F32))
    a = jnp.exp(log_a)
    b = jnp.sqrt(-jnp.expm1(2.0 * log_a)) * (i_gate * xc.astype(F32))

    def combine(left, right):
        a1, b1 = left
        a2, b2 = right
        return a1 * a2, a2 * b1 + b2

    _, hs = lax.associative_scan(combine, (a, b), axis=1)
    return (hs.astype(h.dtype) * jax.nn.gelu(yb)) @ w_out

def band_mask(nblk):
    n = jnp.arange(nblk)[:, None, None]
    i = jnp.arange(BLOCK)[None, :, None]
    j = jnp.arange(2 * BLOCK)[None, None, :]
    s = n * BLOCK - BLOCK + j
    d = n * BLOCK + i - s
    return (d >= 0) & (d < WINDOW) & (s >= 0)

def shared_kv(x, c_act, kv_norm, kv_ada_w, kv_ada_b, w_kv, k_norm, cos, sin):
    bsz, seq, _ = x.shape
    shift, scale = jnp.split(c_act @ kv_ada_w + kv_ada_b, 2, axis=-1)
    h = modulate(x, kv_norm, shift, scale)
    k, v = jnp.split(h @ w_kv, 2, axis=-1)
    k = k.reshape(bsz, seq, N_KV_HEADS, HEAD_DIM)
    v = v.reshape(bsz, seq, N_KV_HEADS, HEAD_DIM)
    k = rotary(rms_norm(k, k_norm), cos, sin)
    nblk = seq // BLOCK

    def to_windows(t):
        tb = t.reshape(bsz, nblk, BLOCK, N_KV_HEADS, HEAD_DIM).transpose(1, 0, 2, 3, 4)
        prev = jnp.concatenate([jnp.zeros_like(tb[:1]), tb[:-1]], axis=0)
        return jnp.concatenate([prev, tb], axis=2)

    return to_windows(k), to_windows(v)

def swa_sink_attention(h, w_q, q_norm, sinks, w_o, k_win, v_win, mask, cos, sin):
    bsz, seq, _ = h.shape
    nblk = seq // BLOCK
    q = (h @ w_q).reshape(bsz, seq, N_Q_HEADS, HEAD_DIM)
    q = rotary(rms_norm(q, q_norm), cos, sin)
    qb = q.reshape(bsz, nblk, BLOCK, N_KV_HEADS, GROUP, HEAD_DIM).transpose(1, 0, 2, 3, 4, 5)
    sink = sinks.astype(F32).reshape(N_KV_HEADS, GROUP)
    scale = HEAD_DIM ** -0.5

    def block_attn(args):
        qi, ki, vi, mi = args
        s = jnp.einsum('bqkgd,bskd->bkgqs', qi, ki).astype(F32) * scale
        s = jnp.where(mi[None, None, None], s, -jnp.inf)
        sink_col = jnp.broadcast_to(sink[None, :, :, None, None], s.shape[:-1] + (1,))
        p = jax.nn.softmax(jnp.concatenate([s, sink_col], axis=-1), axis=-1)[..., :-1]
        return jnp.einsum('bkgqs,bskd->bqkgd', p.astype(vi.dtype), vi)

    o = lax.map(block_attn, (qb, k_win, v_win, mask))
    o = o.transpose(1, 0, 2, 3, 4, 5).reshape(bsz, seq, N_Q_HEADS * HEAD_DIM)
    return o @ w_o

def swiglu(h, w_gu, w_down):
    g, u = jnp.split(h @ w_gu, 2, axis=-1)
    return (jax.nn.silu(g) * u) @ w_down

def moe_swiglu(h, w_router, w_gu, w_down):
    bsz, seq, d = h.shape
    t = h.reshape(-1, d)
    logits = (t @ w_router).astype(F32)
    top_v, top_i = lax.top_k(logits, TOP_K)
    top_w = jax.nn.softmax(top_v, axis=-1)
    gates = jnp.sum(jax.nn.one_hot(top_i, N_EXPERTS, dtype=F32) * top_w[..., None], axis=1)
    out = jnp.zeros_like(t)
    for e in range(N_EXPERTS):
        out = out + gates[:, e:e + 1].astype(t.dtype) * swiglu(t, w_gu[e], w_down[e])
    return out.reshape(bsz, seq, d)

def setup_inputs(seed: int = 0) -> dict:
    key = jax.random.key(seed)
    ks = iter(jax.random.split(key, 40))
    nrm = lambda shape, s: jax.random.normal(next(ks), shape, F32) * s
    gain = lambda shape: 1.0 + 0.05 * jax.random.normal(next(ks), shape, F32)
    D = D_MODEL
    x = nrm((BATCH, SEQ, D), 1.0)
    c = nrm((BATCH, D), 1.0)
    offs = jax.random.randint(next(ks), (BATCH, 1), 0, 1024, dtype=jnp.int32)
    positions = (offs + jnp.arange(SEQ, dtype=jnp.int32)[None, :]).astype(jnp.int32)
    ada_w = nrm((DEPTH, D, 6 * D), 0.1 * D ** -0.5)
    ada_b = nrm((DEPTH, 6 * D), 0.02)
    mix_norm = gain((DEPTH, D))
    ffn_norm = gain((DEPTH, D))
    a_w_in = nrm((N_A_LAYERS, D, 2 * D_RNN), D ** -0.5)
    a_conv_w = nrm((N_A_LAYERS, CONV_W, D_RNN), CONV_W ** -0.5)
    a_conv_b = nrm((N_A_LAYERS, D_RNN), 0.02)
    a_gx_w = nrm((N_A_LAYERS, RNN_BLOCKS, RNN_BLOCK_W, RNN_BLOCK_W), RNN_BLOCK_W ** -0.5)
    a_gx_b = nrm((N_A_LAYERS, D_RNN), 0.02)
    a_ga_w = nrm((N_A_LAYERS, RNN_BLOCKS, RNN_BLOCK_W, RNN_BLOCK_W), RNN_BLOCK_W ** -0.5)
    a_ga_b = nrm((N_A_LAYERS, D_RNN), 0.02)
    u = jax.random.uniform(next(ks), (N_A_LAYERS, D_RNN), F32, 0.9, 0.999)
    sig = u ** (1.0 / LRU_C)
    a_lambda = jnp.log(sig) - jnp.log1p(-sig)
    a_w_out = nrm((N_A_LAYERS, D_RNN, D), D_RNN ** -0.5)
    kv_norm = gain((D,))
    kv_ada_w = nrm((D, 2 * D), 0.1 * D ** -0.5)
    kv_ada_b = nrm((2 * D,), 0.02)
    w_kv = nrm((D, 2 * N_KV_HEADS * HEAD_DIM), D ** -0.5)
    k_norm = gain((HEAD_DIM,))
    b_w_q = nrm((N_B_LAYERS, D, N_Q_HEADS * HEAD_DIM), D ** -0.5)
    b_q_norm = gain((N_B_LAYERS, HEAD_DIM))
    b_sinks = nrm((N_B_LAYERS, N_Q_HEADS), 1.0)
    b_w_o = nrm((N_B_LAYERS, N_Q_HEADS * HEAD_DIM, D), (N_Q_HEADS * HEAD_DIM) ** -0.5)
    f_w_gu = nrm((N_DENSE, D, 2 * D_FF), D ** -0.5)
    f_w_down = nrm((N_DENSE, D_FF, D), D_FF ** -0.5)
    m_router = nrm((N_MOE, D, N_EXPERTS), D ** -0.5)
    m_w_gu = nrm((N_MOE, N_EXPERTS, D, 2 * D_FF_EXPERT), D ** -0.5)
    m_w_down = nrm((N_MOE, N_EXPERTS, D_FF_EXPERT, D), D_FF_EXPERT ** -0.5)
    return {"x": x, "c": c, "positions": positions, "ada_w": ada_w, "ada_b": ada_b,
            "mix_norm": mix_norm, "ffn_norm": ffn_norm, "a_w_in": a_w_in, "a_conv_w": a_conv_w,
            "a_conv_b": a_conv_b, "a_gx_w": a_gx_w, "a_gx_b": a_gx_b, "a_ga_w": a_ga_w,
            "a_ga_b": a_ga_b, "a_lambda": a_lambda, "a_w_out": a_w_out, "kv_norm": kv_norm,
            "kv_ada_w": kv_ada_w, "kv_ada_b": kv_ada_b, "w_kv": w_kv, "k_norm": k_norm,
            "b_w_q": b_w_q, "b_q_norm": b_q_norm, "b_sinks": b_sinks, "b_w_o": b_w_o,
            "f_w_gu": f_w_gu, "f_w_down": f_w_down, "m_router": m_router, "m_w_gu": m_w_gu,
            "m_w_down": m_w_down}

def reference(x, c, positions, ada_w, ada_b, mix_norm, ffn_norm, a_w_in, a_conv_w, a_conv_b,
              a_gx_w, a_gx_b, a_ga_w, a_ga_b, a_lambda, a_w_out, kv_norm, kv_ada_w, kv_ada_b,
              w_kv, k_norm, b_w_q, b_q_norm, b_sinks, b_w_o, f_w_gu, f_w_down, m_router,
              m_w_gu, m_w_down):
    cos, sin = rope_tables(positions, x.dtype)
    c_act = jax.nn.silu(c)
    mask = band_mask(x.shape[1] // BLOCK)
    k_win = None
    v_win = None
    for l in range(DEPTH):
        mod = c_act @ ada_w[l] + ada_b[l]
        sh1, sc1, g1, sh2, sc2, g2 = jnp.split(mod, 6, axis=-1)
        if l < N_A_LAYERS:
            h = modulate(x, mix_norm[l], sh1, sc1)
            y = rglru_mixer(h, a_w_in[l], a_conv_w[l], a_conv_b[l], a_gx_w[l], a_gx_b[l],
                            a_ga_w[l], a_ga_b[l], a_lambda[l], a_w_out[l])
        else:
            if l == N_A_LAYERS:
                k_win, v_win = shared_kv(x, c_act, kv_norm, kv_ada_w, kv_ada_b, w_kv, k_norm, cos, sin)
            bi = l - N_A_LAYERS
            h = modulate(x, mix_norm[l], sh1, sc1)
            y = swa_sink_attention(h, b_w_q[bi], b_q_norm[bi], b_sinks[bi], b_w_o[bi],
                                   k_win, v_win, mask, cos, sin)
        x = x + (1 + g1[:, None, :]) * y
        h = modulate(x, ffn_norm[l], sh2, sc2)
        if l % 2 == 0:
            y = swiglu(h, f_w_gu[l // 2], f_w_down[l // 2])
        else:
            y = moe_swiglu(h, m_router[l // 2], m_w_gu[l // 2], m_w_down[l // 2])
        x = x + (1 + g2[:, None, :]) * y
    return x


_drawn_inputs = setup_inputs


def setup_inputs(seed=0):
    import zlib

    import numpy as np

    out = dict(_drawn_inputs(seed))
    spreads = {}
    factors = {'a_gx_b': 4.029, 'a_ga_b': 19.016, 'b_sinks': 21.918, 'k_norm': 3.33, 'b_q_norm': 8.0}
    for name, (base, spread) in spreads.items():
        noise = np.random.default_rng([zlib.crc32(name.encode()), seed]).standard_normal(out[name].shape)
        drawn = base * np.exp(spread * noise) if base else spread * noise
        out[name] = __import__('jax').numpy.asarray(drawn.astype(out[name].dtype))
    for name, factor in factors.items():
        out[name] = (out[name] * factor).astype(out[name].dtype)
    return out
```

```python
import math
from contextlib import ExitStack

import concourse.bass as bass
from concourse import mybir

F32 = mybir.dt.float32
I32 = mybir.dt.int32
F32R = mybir.dt.float32r
ALU = mybir.AluOpType
ACT = mybir.ActivationFunctionType
AX = mybir.AxisListType

P = 128
D = 1024
SEQ = 256
KC = D // P
NB = SEQ // P
D_FF = 3 * D
FE = 7 * D // 2
E = 8
HD = 64
NH = D // HD
NKV = 4
EPS = 1e-6
LRU_C = 8.0
CAP = 128
NBLK = -(-SEQ // CAP)
RING = 5
WB = 4
SLOT = 6144
UC = 512
PAIRS_DENSE = D_FF // (2 * P)
PAIRS = FE // (2 * P)
STEPS = 6 * PAIRS
NEG = -1e30
TWO_PI = (6.28125, 0.0019350051879882812, 3.019916050561733e-07)


class Signal:

    def __init__(self, sem):
        self.sem, self.n = sem, 0

    def up(self, ins):
        ins.then_inc(self.sem, 1)
        self.n += 1


def build(nc, x, c, positions, inv_freq, ada_w, ada_b, mix_norm, ffn_norm, a_w_in, a_conv_w, a_conv_b,
          a_gx_w, a_gx_b, a_ga_w, a_ga_b, a_lambda, a_w_out, kv_norm, kv_ada_w, kv_ada_b, w_kv,
          k_norm, b_w_q, b_q_norm, b_sinks, b_w_o, f_w_gu, f_w_down, m_router, m_w_gu, m_w_down, out):
    ctx = ExitStack()
    with ctx:
        def sb(name, shape, dt=F32):
            return ctx.enter_context(nc.sbuf_tensor(name, shape, dt))

        def sem(name):
            return ctx.enter_context(nc.semaphore(name))

        ring = [sb(f"ring{i}", [P, SLOT]) for i in range(RING)]
        xT = sb("xT", [P, KC, SEQ])
        A = sb("A", [P, KC, SEQ])
        cols = sb("cols", [P, 224])
        mod = sb("mod", [P, 112])
        aff = sb("aff", [P, 40])
        gate1 = sb("gate1", [P, 32])
        cact = sb("cact", [P, 8])
        lru = sb("lru", [P, 8, 8])
        s8 = lru[:, 7, :]
        eps = sb("eps", [P, 1])
        ident = sb("ident", [P, P])
        ones = sb("ones", [P, P])
        mean_w = sb("mean_w", [P, P])
        before = sb("before", [P, P])
        mask = sb("mask", [P, 3 * P])
        iota = sb("iota", [P, NBLK * CAP])
        rms = sb("rms", [P, SEQ])
        rstd = sb("rstd", [P, SEQ])
        silu = sb("silu", [P, 2, SEQ])
        lt = silu
        pos_i = sb("pos_i", [P, NB], I32)
        ang = sb("ang", [P, NB, HD // 2])
        turn = sb("turn", [P, NB, HD // 2])
        turn_i = sb("turn_i", [P, NB, HD // 2], I32)
        posf = sb("posf", [P, NB])
        inv_bc = sb("inv_bc", [P, HD // 2])
        cos2 = sb("cos2", [P, NB, HD])
        sin2 = sb("sin2", [P, NB, HD])
        kg = sb("kg", [P, HD])
        qg = sb("qg", [P, HD])
        sinks = sb("sinks", [P, NH])
        half_pi = sb("half_pi", [P, 1])
        ssq = sb("ssq", [P, 2, 8])
        mx = sb("mx", [P, NH, 2])
        nm = sb("nm", [P, NH, 2])
        sm = sb("sm", [P, NH, 2])
        es = sb("es", [P, NH, 2])
        rt_w = sb("rt_w", [P, KC, E])
        rt = sb("rt", [P, 12, NB, E + 1])
        rts = sb("rts", [P, 8, NB])
        cnt_i = sb("cnt_i", [P, E], I32)
        bank = [ctx.enter_context(nc.psum_tensor(f"bank{i}", [P, 512], F32)) for i in range(8)]

        with ExitStack() as region:
            def shared(name, shape, dt=F32):
                return region.enter_context(nc.sbuf_tensor(name, shape, dt))

            H = shared("H", [P, KC, SEQ])
            B = shared("B", [P, KC, SEQ])
            C = shared("C", [P, KC, SEQ])
            Dd = shared("Dd", [P, KC, SEQ])
            hid = shared("hid", [P, 2, 2, SEQ])
            sqb = shared("sqb", [P, 2, UC])
            qw = shared("qw", [P, 2, UC])
            rtmp = shared("rtmp", [P, UC])
            kT = shared("kT", [P, NKV, SEQ])
            vt = shared("vt", [P, NB, NKV * HD])
            PT = shared("PT", [P, 2, 3 * P])
        with ExitStack() as region:
            whi = shared("whi", [P, WB, 1024], F32R)
            wlo = shared("wlo", [P, WB, 1024], F32R)
            xh = shared("xh", [P, KC, CAP], F32R)
            xl = shared("xl", [P, KC, CAP], F32R)
            hs = shared("hs", [P, 2, 2 * P])
            hh = shared("hh", [P, 2, 2, CAP], F32R)
            hl = shared("hl", [P, 2, 2, CAP], F32R)
            y = shared("y", [CAP, D])
            sel = shared("sel", [P, NB, CAP])
            selg = shared("selg", [P, NB, CAP])
            selT = shared("selT", [CAP, SEQ])
        iota_i = rtmp[:, 0:NBLK * CAP].bitcast(I32)
        kdup = hid[:, :, :, :].rearrange("p a i n -> p (a i n)").rearrange("p (b h t d) -> p b h t d", b=NB, h=NKV, t=2)
        pa_rows, pb_rows = B[:, 0, 0:P], B[:, 0, P:2 * P]
        Pb = Dd[:, :, :].rearrange("p k n -> p (k n)")[:, 0:4 * 3 * P].rearrange("p (b n) -> p b n", b=4)
        htok = A[:, :, :].rearrange("p k n -> p (k n)").rearrange("p (b n) -> p b n", b=NB)
        xin = Dd[:, :, :].rearrange("p k n -> p (k n)").rearrange("p (b n) -> p b n", b=NB)
        otok = A[:, :, :].rearrange("p k n -> p (k n)").rearrange("p (b n) -> p b n", b=NB)
        gates, pos, msk = rt[:, 9, :, 0:E], rt[:, 10, :, 0:E], rt[:, 11, :, 0:E]

        CA_BIAS, CA_MIX = 0, 112
        CB = P
        CB_FFN, CB_KVN, CB_CONVW, CB_CONVB, CB_GXB, CB_GAB, CB_LAM, CB_C = (
            CB, CB + 16, CB + 24, CB + 56, CB + 64, CB + 72, CB + 80, CB + 88)
        NB_ROWS = 96

        par_in = sem("par_in")
        x_in = sem("x_in")
        misc_in = sem("misc_in")
        ring_full = [sem(f"ring_full{i}") for i in range(RING)]
        out_stored = sem("out_stored")
        consts = sem("consts")
        par_tp = sem("par_tp")
        cols_ready = sem("cols_ready")
        x_tp = sem("x_tp")
        acc_full = [sem(f"acc_full{b}") for b in range(2)]
        acc_free = [sem(f"acc_free{b}") for b in range(2)]
        ada_mm = sem("ada_mm")
        ada_done = sem("ada_done")
        cact_ready = sem("cact_ready")
        mod_ready = sem("mod_ready")
        dve_step = sem("dve_step")
        act_step = sem("act_step")
        x_new = sem("x_new")
        sq_done = sem("sq_done")
        stat_mm = sem("stat_mm")
        rms_done = sem("rms_done")
        xn_done = sem("xn_done")
        h_done = sem("h_done")
        conv_done = sem("conv_done")
        lam_a = sem("lam_a")
        lam_d = sem("lam_d")
        lru_a = sem("lru_a")
        lru_var = sem("lru_var")
        lru_beta = sem("lru_beta")
        mix_done = sem("mix_done")
        silu_done = sem("silu_done")
        hid_done = sem("hid_done")
        down_mm = sem("down_mm")
        rope_a = sem("rope_a")
        rope_d = sem("rope_d")
        qsq_done = sem("qsq_done")
        ss_done = sem("ss_done")
        rq_done = sem("rq_done")
        rope_done = sem("rope_done")
        qk_tp = sem("qk_tp")
        qkT_done = sem("qkT_done")
        sc_mm = sem("sc_mm")
        sc_evac = sem("sc_evac")
        nm_done = sem("nm_done")
        exp_done = sem("exp_done")
        pn_done = sem("pn_done")
        pT_mm = sem("pT_mm")
        pT_evac = sem("pT_evac")
        pv_mm = sem("pv_mm")
        o_evac = sem("o_evac")
        rt_mm = sem("rt_mm")
        mask_ready = sem("mask_ready")
        pos_mm = sem("pos_mm")
        cnt_ready = sem("cnt_ready")
        rt_a = sem("rt_a")
        rt_d = sem("rt_d")
        ht_tp = sem("ht_tp")
        ht_done = sem("ht_done")
        sel_ready = sem("sel_ready")
        xg_mm = sem("xg_mm")
        xh_ready = sem("xh_ready")
        xl_ready = sem("xl_ready")
        selg_ready = sem("selg_ready")
        selT_mm = sem("selT_mm")
        selT_ready = sem("selT_ready")
        hi_ready = sem("hi_ready")
        lo_ready = sem("lo_ready")
        step_used = sem("step_used")
        silu_ready = sem("silu_ready")
        hs_ready = sem("hs_ready")
        hT_mm = sem("hT_mm")
        hh_ready = sem("hh_ready")
        hl_ready = sem("hl_ready")
        y_a = sem("y_a")
        y_d = sem("y_d")
        back_mm = sem("back_mm")
        back_done = sem("back_done")
        x_final = sem("x_final")
        fin_tp = sem("fin_tp")
        fin_evac = sem("fin_evac")

        def cols_of(w, c0):
            src = w.rearrange("(k p) n -> p k n", p=P)[:, :, c0:c0 + UC]
            return [(lambda s: s[:, 0:KC * UC].rearrange("p (k n) -> p k n", k=KC), src)]

        def pair_of(gu, down, ff, t):
            f0 = 2 * P * t
            g = gu.rearrange("(k p) n -> p k n", p=P)
            return [
                (lambda s: s[:, 0:2048].rearrange("p (k n) -> p k n", k=KC), g[:, :, f0:f0 + 2 * P]),
                (lambda s: s[:, 2048:4096].rearrange("p (k n) -> p k n", k=KC), g[:, :, ff + f0:ff + f0 + 2 * P]),
                (lambda s: s[:, 4096:6144].rearrange("p (i n) -> p i n", i=2),
                 down[f0:f0 + 2 * P, :].rearrange("(i p) n -> p i n", p=P)),
            ]

        def expert_pair_of(gu, down, t):
            f0 = 2 * P * t
            g = gu.rearrange("(k p) n -> p k n", p=P)
            side = lambda s: s[:, 0:4096].rearrange("p (k h n) -> p k h n", k=KC, h=2)
            return [
                (lambda s: side(s)[:, :, 0, :], g[:, :, f0:f0 + 2 * P]),
                (lambda s: side(s)[:, :, 1, :], g[:, :, FE + f0:FE + f0 + 2 * P]),
                (lambda s: s[:, 4096:6144].rearrange("p (i n) -> p i n", i=2),
                 down[f0:f0 + 2 * P, :].rearrange("(i p) n -> p i n", p=P)),
            ]

        units, name_of, last_use = [], {}, []

        def unit(name, parts, used_by):
            name_of[name] = len(units)
            units.append(parts)
            last_use.append(used_by)

        def task_end(T):
            return acc_full[T % 2], ACC_FULL_AT[T]

        ACC_FULL_AT = {T: T // 2 + 1 for T in range(54)}

        def ada_unit(v):
            w, v0 = (ada_w[0], 0) if v < 12 else (kv_ada_w, 12) if v < 16 else (ada_w[1], 16)
            unit(("ada", v), cols_of(w, (v - v0) * UC), (ada_mm, v + 1))

        for v in range(4):
            ada_unit(v)
        for i in range(4):
            unit(("in", i), cols_of(a_w_in[0], i * UC), task_end(2 * i + 1))
        unit("gates", [
            (lambda s: s[:, 0:1024].rearrange("p (k n) -> p k n", k=8), a_ga_w[0].rearrange("b c d -> c b d")),
            (lambda s: s[:, 1024:2048].rearrange("p (k n) -> p k n", k=8), a_gx_w[0].rearrange("b c d -> c b d"))],
            task_end(15))
        for v in range(4, 10):
            ada_unit(v)
        for i in range(2):
            unit(("out", i), cols_of(a_w_out[0], i * UC), task_end(17 + 2 * i))
        for t in range(PAIRS_DENSE):
            unit(("ff", t), pair_of(f_w_gu[0], f_w_down[0], D_FF, t), (down_mm, t + 1))
            if t < 10:
                ada_unit(10 + t)
        unit("kv", cols_of(w_kv, 0), task_end(45))
        for i in range(2):
            unit(("q", i), cols_of(b_w_q[0], i * UC), task_end(47 + 2 * i))
        for v in range(20, 28):
            ada_unit(v)
        for i in range(2):
            unit(("o", i), cols_of(b_w_o[0], i * UC), task_end(51 + 2 * i))
        U0 = len(units)
        full_at, sofar = [], [0] * RING
        for u in range(U0):
            s = (u - U0) % RING
            sofar[s] += 16 * len(units[u])
            full_at.append((s, sofar[s]))
        uses = [len(range(s, PAIRS, RING)) for s in range(RING)]
        read_at = [6 * t + 10 if t < PAIRS - 1 else STEPS for t in range(PAIRS)]
        freed_at = [read_at[t - RING] if t >= RING else read_at[max(range(t, PAIRS, RING))] - STEPS
                    for t in range(PAIRS)]
        moe_full = [(t % RING, sofar[t % RING] + 48 * (t // RING + 1), 48 * uses[t % RING]) for t in range(PAIRS)]

        acc_tasks = 54

        ACC_FREE_AT = {T: T // 2 + 1 for T in range(16)} | {T: 9 + (T - 44) // 2 for T in range(44, 50)}

        def after(eng, sem, v):
            if not isinstance(v, int) or v > 0:
                eng.wait_ge(sem, v)

        def wait_free(eng, T):
            if 16 <= T < 20:
                eng.wait_ge(x_new, 4 + T - 16 + 1)
            elif 20 <= T < 44:
                eng.wait_ge(hid_done, T - 20 + 1)
            elif T >= 50:
                eng.wait_ge(x_new, 12 + T - 50 + 1)
            else:
                eng.wait_ge(acc_free[T % 2], ACC_FREE_AT[T])

        def more_jobs(eng, job, **how):
            reg = eng.alloc_register(f"job_{eng.engine.name}")
            eng.reg_mov(reg, E)
            with eng.Fori(0, E) as e:
                n = eng.value_load(cnt_i[0:1, bass.ds(e, 1)], min_val=0, max_val=SEQ)
                for b in range(1, NBLK):
                    with eng.If(n > b * CAP):
                        j = eng.snap(reg, min_val=E, max_val=E * NBLK)
                        job(j, e, b, **how)
                        eng.reg_add(reg, reg, 1)

        def step_order():
            for t in range(PAIRS + 1):
                for part in range(4 if t < PAIRS else 0):
                    yield t, part
                for part in range(4, 6 if t else 4):
                    yield t - 1, part

        def raw(t, part):
            return ring[t % RING][:, 1024 * part:1024 * (part + 1)]

        CONSTS = 12

        block = ctx.enter_context(nc.Block())

        @block.sync
        def _(sp):
            for u, parts in enumerate(units):
                s = full_at[u][0]
                if u >= RING:
                    sp.wait_ge(*last_use[u - RING])
                for dst, src in parts:
                    sp.dma_start(dst(ring[s]), src).then_inc(ring_full[s], 16)
                if u == 0:
                    sp.dma_start(xin[:, 0:NB, :], x[0].rearrange("(b p) n -> p b n", p=P)).then_inc(x_in, 16)

            def job(j, e, blk=0):
                gu = m_w_gu[0][bass.ds(e, 1)].rearrange("o r n -> (o r) n")
                down = m_w_down[0][bass.ds(e, 1)].rearrange("o r n -> (o r) n")
                for t in range(PAIRS):
                    if isinstance(j, int) and t < RING:
                        sp.wait_ge(*last_use[U0 + t - RING])
                    else:
                        sp.wait_ge(lo_ready, j * STEPS + freed_at[t])
                    for dst, src in expert_pair_of(gu, down, t):
                        sp.dma_start(dst(ring[t % RING]), src).then_inc(ring_full[t % RING], 16)

            job(0, 0)
            with sp.Fori(1, E) as e:
                job(e, e)
            sp.wait_ge(cnt_ready, 1)
            more_jobs(sp, job)
            for n in range(NB):
                sp.wait_ge(fin_evac, 2 * n + 2)
                sp.dma_start(out[0][n * P:(n + 1) * P, :], otok[:, n, :]).then_inc(out_stored, 16)
            sp.wait_ge(out_stored, 16 * NB)

        @block.gpsimd
        def _(pool):
            made = Signal(consts)

            def do(ins):
                made.up(ins)
                pool.wait_ge(consts, made.n)

            do(nc.gpsimd.memset(eps[:, :], EPS))
            do(nc.gpsimd.memset(half_pi[:, :], math.pi / 2))
            do(nc.gpsimd.memset(ones[:, :], 1.0))
            do(nc.gpsimd.memset(mean_w[:, :], 1.0 / D))
            do(nc.gpsimd.affine_select(out=ident[:, :], in_=ones[:, :], compare_op=ALU.is_equal, fill=0.0, base=0,
                                       pattern=[[-1, P]], channel_multiplier=1))
            do(nc.gpsimd.affine_select(out=before[:, :], in_=ones[:, :], compare_op=ALU.is_gt, fill=0.0, base=0,
                                       pattern=[[1, P]], channel_multiplier=-1))
            do(nc.gpsimd.memset(mask[:, :], 0.0))
            for i, (sign, op) in enumerate(((1, ALU.is_ge), (-1, ALU.is_gt), (1, ALU.is_ge))):
                m = mask[:, i * P:(i + 1) * P]
                do(nc.gpsimd.affine_select(out=m, in_=m, compare_op=op, fill=NEG, base=0,
                                           pattern=[[-sign, P]], channel_multiplier=sign))
            do(nc.gpsimd.iota(iota_i[:, :], pattern=[[1, NBLK * CAP]], base=0, channel_multiplier=0))
            do(nc.gpsimd.tensor_copy(iota[:, :], iota_i[:, :]))
            assert made.n == CONSTS

        @block.scalar
        def _(act):
            step = Signal(act_step)

            def then(ins, signal=None):
                s = signal or step
                s.up(ins)
                act.wait_ge(s.sem, s.n)

            rows = [(pa_rows, 0, ada_b[0]), (pa_rows, 48, kv_ada_b), (pa_rows, 64, ada_b[1]),
                    (pa_rows, 112, mix_norm.rearrange("l n -> (l n)")), (pb_rows, 0, ffn_norm.rearrange("l n -> (l n)")),
                    (pb_rows, 16, kv_norm), (pb_rows, 24, a_conv_w[0].rearrange("l n -> (l n)")),
                    (pb_rows, 56, a_conv_b[0]), (pb_rows, 64, a_gx_b[0]), (pb_rows, 72, a_ga_b[0]),
                    (pb_rows, 80, a_lambda[0]), (pb_rows, 88, c[0])]
            for dst, r, src in rows:
                v = src.rearrange("(r n) -> r n", n=P)
                act.dma_start(dst[r:r + v.shape[0], :], v).then_inc(par_in, 16)
            with nc.allow_non_contiguous_dma(reason="256 positions, one per partition"):
                act.dma_start(pos_i[:, :], positions[0].rearrange("(b p) -> p b", p=P)).then_inc(misc_in, 16)
            act.dma_start(inv_bc[:, :], inv_freq.to_broadcast([P, HD // 2])).then_inc(misc_in, 16)
            act.dma_start(kg[:, :], k_norm[None, :].to_broadcast([P, HD])).then_inc(misc_in, 16)
            act.dma_start(qg[:, :], b_q_norm.to_broadcast([P, HD])).then_inc(misc_in, 16)
            act.dma_start(sinks[:, :], b_sinks.to_broadcast([P, NH])).then_inc(misc_in, 16)
            act.dma_start(rt_w[:, :, :], m_router[0].rearrange("(k p) e -> p k e", p=P)).then_inc(misc_in, 16)

            act.wait_ge(consts, CONSTS)
            act.wait_ge(cols_ready, 1)
            then(nc.scalar.activation(cact[:, :], cols[:, CB_C:CB_C + 8], ACT.Silu), Signal(cact_ready))
            la = Signal(lam_a)
            then(nc.scalar.activation(lru[:, 0, :], cols[:, CB_LAM:CB_LAM + 8], ACT.Abs), la)
            then(nc.scalar.activation(lru[:, 1, :], lru[:, 0, :], ACT.Exp, scale=-1.0), la)
            act.wait_ge(lam_d, 1)
            then(nc.scalar.activation(lru[:, 3, :], lru[:, 2, :], ACT.Ln), la)

            h_sig, sqs, rmss = Signal(h_done), Signal(sq_done), Signal(rms_done)

            def norm(q, affines):
                for i in range(4):
                    act.wait_ge(x_new, 4 * q + i + 1)
                    then(nc.scalar.activation(B[:, 2 * i:2 * i + 2, :], xT[:, 2 * i:2 * i + 2, :], ACT.Square), sqs)
                act.wait_ge(stat_mm, q + 1)
                then(nc.scalar.activation(rms[:, :], bank[4][:, 0:SEQ], ACT.Sqrt, bias=eps[:, 0:1]), rmss)
                act.wait_ge(mod_ready, q + 1)
                for dst, a0, sh0 in affines:
                    for k in range(KC):
                        act.wait_ge(xn_done, 4 * q + k // 2 + 1)
                        then(nc.scalar.activation(dst[:, k, :], A[:, k, :], ACT.Identity, scale=aff[:, a0 + k:a0 + k + 1],
                                                  bias=mod[:, sh0 + k:sh0 + k + 1]), h_sig)

            norm(0, [(H, 0, 0)])
            for T in range(4, 8):
                act.wait_ge(acc_full[T % 2], T // 2 + 1)
                i = T - 4
                ins = nc.scalar.activation(B[:, 2 * i:2 * i + 2, :], bank[T % 2][:, :].rearrange("p (a n) -> p a n", a=2),
                                           ACT.Gelu_apprx_tanh)
                ins.then_inc(acc_free[T % 2], 1)
                act.wait_ge(acc_free[T % 2], T // 2 + 1)
            for k in range(KC):
                T = 8 + k
                act.wait_ge(acc_full[T % 2], T // 2 + 1)
                then(nc.scalar.activation(A[:, k, :], bank[T % 2][:, 0:SEQ], ACT.Sigmoid,
                                          bias=cols[:, CB_GAB + k:CB_GAB + k + 1]))
                ins = nc.scalar.activation(H[:, k, :], bank[T % 2][:, SEQ:2 * SEQ], ACT.Sigmoid,
                                           bias=cols[:, CB_GXB + k:CB_GXB + k + 1])
                ins.then_inc(acc_free[T % 2], 1)
                act.wait_ge(acc_free[T % 2], T // 2 + 1)
            act.wait_ge(lam_d, 2)
            ls = Signal(lru_a)
            for k in range(KC):
                then(nc.scalar.activation(Dd[:, k, :], A[:, k, :], ACT.Tanh, scale=s8[:, k:k + 1]))
            for k in range(KC):
                then(nc.scalar.activation(A[:, k, :], A[:, k, :], ACT.Exp, scale=s8[:, k:k + 1]), ls)
            bt = Signal(lru_beta)
            for k in range(KC):
                act.wait_ge(lru_var, k + 1)
                then(nc.scalar.activation(Dd[:, k, :], Dd[:, k, :], ACT.Sqrt, scale=-1.0), bt)

            norm(1, [(H, 8, 24)])
            sl = Signal(silu_done)
            for n in range(2 * PAIRS_DENSE):
                T = 20 + n
                act.wait_ge(acc_full[T % 2], T // 2 + 1)
                then(nc.scalar.activation(silu[:, n % 2, :], bank[T % 2][:, 0:SEQ], ACT.Silu), sl)
            ra = Signal(rope_a)
            act.wait_ge(rope_d, 1)
            then(nc.scalar.activation(sin2[:, :, 32:64], ang[:, :, :], ACT.Sin), ra)
            then(nc.scalar.activation(turn[:, :, :], ang[:, :, :], ACT.Abs), ra)
            then(nc.scalar.activation(cos2[:, :, 0:32], turn[:, :, :], ACT.Sin, scale=-1.0, bias=half_pi[:, 0:1]), ra)

            norm(2, [(H, 16, 48), (C, 24, 64)])
            qs, rq, qk = Signal(qsq_done), Signal(rq_done), Signal(qkT_done)

            def squares(T):
                w = 256 if T < 2 else UC
                a = 44 + T
                act.wait_ge(acc_full[a % 2], a // 2 + 1)
                if T >= 2:
                    act.wait_ge(ss_done, T - 1)
                then(nc.scalar.activation(sqb[:, T % 2, 0:w], bank[a % 2][:, 0:w], ACT.Square), qs)

            def roots(T):
                nh = 4 if T < 2 else 8
                act.wait_ge(ss_done, T + 1)
                then(nc.scalar.activation(ssq[:, T % 2, 0:nh], ssq[:, T % 2, 0:nh], ACT.Sqrt, scale=1.0 / HD,
                                          bias=eps[:, 0:1]), rq)

            def copy_T(T):
                act.wait_ge(qk_tp, T + 1)
                dst = kT if T < 2 else B
                c0, n = (0, T) if T < 2 else (4 * ((T - 2) // 2), T % 2)
                then(nc.scalar.activation(dst[:, c0:c0 + 4, n * P:(n + 1) * P],
                                          bank[5 + T % 2][:, :].rearrange("p (a n) -> p a n", a=4), ACT.Copy), qk)

            for T in range(6):
                squares(T)
                roots(T)
                if T:
                    copy_T(T - 1)
            copy_T(5)

            ex, pt, oe = Signal(exp_done), Signal(pT_evac), Signal(o_evac)

            def exps(h):
                act.wait_ge(nm_done, h + 1)
                then(nc.scalar.activation(Pb[:, h % 4, 0:P], Pb[:, h % 4, 0:P], ACT.Exp, bias=nm[:, h, 0:1],
                                          accum_out=sm[:, h, 0:1]))
                then(nc.scalar.activation(Pb[:, h % 4, P:3 * P], Pb[:, h % 4, P:3 * P], ACT.Exp, bias=nm[:, h, 1:2],
                                          accum_out=sm[:, h, 1:2]))
                then(nc.scalar.activation(es[:, h, :], nm[:, h, :], ACT.Exp, bias=sinks[:, h:h + 1]), ex)

            def copy_p(h):
                act.wait_ge(pT_mm, h + 1)
                if h >= 2:
                    act.wait_ge(pv_mm, h - 1)
                then(nc.scalar.activation(PT[:, h % 2, :], bank[7 if h % 2 else 4][:, 0:3 * P], ACT.Copy), pt)

            def copy_o(k):
                act.wait_ge(pv_mm, 2 * k + 2)
                then(nc.scalar.activation(A[:, k, :], bank[k % 2][:, 0:SEQ], ACT.Copy), oe)

            exps(0)
            for h in range(NH):
                if h + 1 < NH:
                    exps(h + 1)
                copy_p(h)
                if h >= 2 and h % 2 == 0:
                    copy_o(h // 2 - 1)
            copy_o(NH // 2 - 1)

            norm(3, [(H, 32, 88)])
            ht = Signal(ht_done)
            for i in range(4):
                act.wait_ge(ht_tp, i + 1)
                then(nc.scalar.activation(htok[:, i // 2, 512 * (i % 2):512 * (i % 2) + 512], bank[6 + i % 2][:, :],
                                          ACT.Copy), ht)
            act.wait_ge(rt_d, 1)
            then(nc.scalar.activation(rts[:, 4, :], rts[:, 3, :], ACT.Exp), Signal(rt_a))

            def take(g):
                act.wait_ge(xg_mm, g + 1)
                for i in range(2):
                    nc.scalar.activation(xh[:, 4 * i:4 * i + 4, :],
                                         bank[6 + i][:, :].rearrange("p (k s) -> p k s", k=4),
                                         ACT.Copy).then_inc(xh_ready, 1)

            def job(j, e, blk=0, extra=False):
                if extra:
                    take(j + 1)
                for n, (t, part) in enumerate(step_order()):
                    if part == 0:
                        s, at, per = moe_full[t]
                        act.wait_ge(ring_full[s], j * per + at)
                    if not (isinstance(j, int) and n < WB):
                        act.wait_ge(step_used, j * STEPS + (n - WB + 1))
                    nc.scalar.activation(whi[:, n % WB, :], raw(t, part), ACT.Copy).then_inc(hi_ready, 1)
                    if (part == 1 and t) or (t == PAIRS - 1 and part == 4):
                        m = t - 1 if part == 1 else t
                        act.wait_ge(step_used, j * STEPS + (6 * m + 2 if m else 4))
                        nc.scalar.activation(silu[:, m % 2, :], bank[m % 2][:, 0:2 * P], ACT.Silu).then_inc(silu_ready, 1)
                    if part == 4 and t < PAIRS - 1:
                        hidden_hi(j, t)
                    if t == 0 and part == 5:
                        act.wait_ge(selT_mm, j + 1)
                        nc.scalar.activation(selT[:, :], bank[3][:, 0:SEQ], ACT.Copy).then_inc(selT_ready, 1)
                if not extra:
                    take(j + 1)
                hidden_hi(j, PAIRS - 1)
                act.wait_ge(step_used, j * STEPS + STEPS)
                nc.scalar.activation(y[:, 0:512], bank[4][:, :], ACT.Copy).then_inc(y_a, 1)

            def hidden_hi(j, t):
                act.wait_ge(hT_mm, j * PAIRS + (t + 1))
                nc.scalar.activation(hh[:, t % 2, :, :], bank[2 + t % 2][:, 0:2 * CAP].rearrange("p (i s) -> p i s", i=2),
                                     ACT.Copy).then_inc(hh_ready, 1)

            take(0)
            job(0, 0)
            with act.Fori(1, E) as e:
                job(e, e)
            act.wait_ge(cnt_ready, 1)
            more_jobs(act, job, extra=True)
            fe = Signal(fin_evac)
            for i in range(4):
                act.wait_ge(fin_tp, i + 1)
                then(nc.scalar.activation(otok[:, i // 2, 512 * (i % 2):512 * (i % 2) + 512], bank[6 + i % 2][:, :],
                                          ACT.Copy), fe)

        @block.vector
        def _(dve):
            step = Signal(dve_step)
            v_ = nc.vector

            def then(ins, signal=None):
                s = signal or step
                s.up(ins)
                dve.wait_ge(s.sem, s.n)

            dve.wait_ge(par_tp, 1)
            then(v_.tensor_copy(cols[:, 0:P + NB_ROWS], bank[5][:, 0:P + NB_ROWS]), Signal(cols_ready))
            xs = Signal(x_new)
            for i in range(4):
                dve.wait_ge(x_tp, i + 1)
                then(v_.tensor_copy(xT[:, 2 * i:2 * i + 2, :],
                                    bank[(0, 1, 6, 7)[i]][:, :].rearrange("p (a n) -> p a n", a=2)), xs)
            ld = Signal(lam_d)
            dve.wait_ge(lam_a, 2)
            then(v_.tensor_scalar(lru[:, 2, :], lru[:, 1, :], 1.0, None, ALU.add), ld)
            then(v_.tensor_scalar(lru[:, 4, :], lru[:, 2, :], -1.0, None, ALU.add))
            then(v_.tensor_scalar(lru[:, 5, :], lru[:, 4, :], 0.0, None, ALU.is_equal))
            then(v_.tensor_tensor(lru[:, 4, :], lru[:, 4, :], lru[:, 5, :], ALU.add))
            then(v_.reciprocal(lru[:, 4, :], lru[:, 4, :]))
            dve.wait_ge(lam_a, 3)
            then(v_.tensor_tensor(lru[:, 4, :], lru[:, 4, :], lru[:, 3, :], ALU.mult))
            then(v_.tensor_tensor(lru[:, 4, :], lru[:, 4, :], lru[:, 5, :], ALU.add))
            then(v_.tensor_tensor(lru[:, 4, :], lru[:, 4, :], lru[:, 1, :], ALU.mult))
            then(v_.tensor_scalar(lru[:, 6, :], cols[:, CB_LAM:CB_LAM + 8], -1.0, 0.0, ALU.mult, ALU.max))
            then(v_.tensor_tensor(lru[:, 4, :], lru[:, 4, :], lru[:, 6, :], ALU.add))
            then(v_.tensor_scalar(s8, lru[:, 4, :], -LRU_C, None, ALU.mult), ld)
            dve.wait_ge(misc_in, 96)
            then(v_.tensor_copy(posf[:, :], pos_i[:, :]))
            for n in range(NB):
                then(v_.tensor_scalar(ang[:, n, :], inv_bc[:, :], posf[:, n:n + 1], None, ALU.mult))
            then(v_.tensor_scalar(turn[:, :, :], ang[:, :, :], 1.0 / (2 * math.pi), None, ALU.mult))
            then(v_.tensor_copy(turn_i[:, :, :], turn[:, :, :]))
            then(v_.tensor_copy(turn[:, :, :], turn_i[:, :, :]))
            for part in TWO_PI:
                then(v_.scalar_tensor_tensor(out=ang[:, :, :], in0=turn[:, :, :], scalar=-part, in1=ang[:, :, :],
                                             op0=ALU.mult, op1=ALU.add))
            for edge, op in ((3.1415925, ALU.min), (-3.1415925, ALU.max)):
                last = v_.tensor_scalar(ang[:, :, :], ang[:, :, :], edge, None, op)
                if op == ALU.min:
                    then(last)
            then(last, Signal(rope_d))

            ad, mr = Signal(ada_done), Signal(mod_ready)

            def affine(a0, sc0, g0, signal=None):
                then(v_.scalar_tensor_tensor(out=aff[:, a0:a0 + 8], in0=mod[:, sc0:sc0 + 8], scalar=1.0,
                                             in1=cols[:, g0:g0 + 8], op0=ALU.add, op1=ALU.mult), signal)

            def gate(i, g0):
                then(v_.tensor_scalar(gate1[:, 8 * i:8 * i + 8], mod[:, g0:g0 + 8], 1.0, None, ALU.add))

            def ada(v):
                dve.wait_ge(ada_mm, v + 1)
                then(v_.tensor_tensor(mod[:, 4 * v:4 * v + 4], bank[2 + v % 2][:, 0:4], cols[:, 4 * v:4 * v + 4],
                                      ALU.add), ad)
                if v == 3:
                    affine(0, 8, CA_MIX, mr)
                elif v == 5:
                    gate(0, 16)
                elif v == 9:
                    affine(8, 32, CB_FFN, mr)
                elif v == 11:
                    gate(1, 40)
                elif v == 15:
                    affine(16, 56, CB_KVN)
                elif v == 19:
                    affine(24, 72, CA_MIX + 8, mr)
                elif v == 21:
                    gate(2, 80)
                elif v == 25:
                    affine(32, 96, CB_FFN + 8, mr)
                elif v == 27:
                    gate(3, 104)

            xn = Signal(xn_done)

            def norm(q):
                dve.wait_ge(rms_done, q + 1)
                then(v_.reciprocal(rstd[:, :], rms[:, :]))
                for i in range(4):
                    then(v_.tensor_tensor(A[:, 2 * i:2 * i + 2, :], xT[:, 2 * i:2 * i + 2, :],
                                          rstd[:, None, :].to_broadcast([P, 2, SEQ]), ALU.mult), xn)

            norm(0)
            for v in range(4):
                ada(v)
            cv = Signal(conv_done)
            for k in range(KC):
                T, half = k // 2, bank[(k // 2) % 2][:, SEQ * (k % 2):SEQ * (k % 2) + SEQ]
                if k % 2 == 0:
                    dve.wait_ge(acc_full[T % 2], T // 2 + 1)
                w = [cols[:, CB_CONVW + 8 * t + k:CB_CONVW + 8 * t + k + 1] for t in range(4)]
                then(v_.tensor_scalar(C[:, k, :], half, w[3], cols[:, CB_CONVB + k:CB_CONVB + k + 1], ALU.mult, ALU.add))
                for lag in (1, 2, 3):
                    ins = v_.scalar_tensor_tensor(out=C[:, k, lag:], in0=half[:, 0:SEQ - lag], scalar=w[3 - lag],
                                                  in1=C[:, k, lag:], op0=ALU.mult, op1=ALU.add)
                    if lag < 3:
                        then(ins)
                    elif k % 2 == 0:
                        then(ins, cv)
                    else:
                        ins.then_inc(acc_free[T % 2], 1)
                        dve.wait_ge(acc_free[T % 2], T // 2 + 1)
            for v in range(4, 6):
                ada(v)
            var, mxd = Signal(lru_var), Signal(mix_done)
            for k in range(KC):
                dve.wait_ge(lru_a, k + 1)
                then(v_.tensor_tensor(lt[:, k % 2, :], A[:, k, :], A[:, k, :], ALU.mult))
                then(v_.scalar_tensor_tensor(out=Dd[:, k, :], in0=lt[:, k % 2, :], scalar=1.0, in1=Dd[:, k, :],
                                             op0=ALU.add, op1=ALU.mult), var)
            for k in range(KC):
                then(v_.tensor_tensor(H[:, k, :], H[:, k, :], C[:, k, :], ALU.mult))
                dve.wait_ge(lru_beta, k + 1)
                then(v_.tensor_tensor(H[:, k, :], H[:, k, :], Dd[:, k, :], ALU.mult))
                then(v_.tensor_tensor_scan(C[:, k, :], A[:, k, :], H[:, k, :], 0.0, ALU.mult, ALU.add))
                then(v_.tensor_tensor(C[:, k, :], C[:, k, :], B[:, k, :], ALU.mult), mxd)
            for v in range(6, 10):
                ada(v)

            def residual(T0, g):
                for T in range(T0, T0 + 4):
                    dve.wait_ge(acc_full[T % 2], T // 2 + 1)
                    for a in range(2):
                        k = 2 * (T - T0) + a
                        ins = v_.scalar_tensor_tensor(out=xT[:, k, :], in0=bank[T % 2][:, SEQ * a:SEQ * a + SEQ],
                                                      scalar=gate1[:, 8 * g + k:8 * g + k + 1], in1=xT[:, k, :],
                                                      op0=ALU.mult, op1=ALU.add)
                        if a == 0:
                            then(ins)
                        else:
                            then(ins, xs)

            residual(16, 0)
            norm(1)
            hd = Signal(hid_done)
            for n in range(2 * PAIRS_DENSE):
                T = 20 + n
                dve.wait_ge(silu_done, n + 1)
                ins = v_.tensor_tensor(hid[:, (n // 2) % 2, n % 2, :], silu[:, n % 2, :],
                                       bank[T % 2][:, SEQ:2 * SEQ], ALU.mult)
                then(ins, hd)
                if n % 2 == 1 and 1 <= n // 2 <= 10:
                    ada(10 + n // 2 - 1)
            dve.wait_ge(down_mm, PAIRS_DENSE)
            for i in range(4):
                for a in range(2):
                    k = 2 * i + a
                    then(v_.scalar_tensor_tensor(out=xT[:, k, :], in0=bank[4 + i][:, SEQ * a:SEQ * a + SEQ],
                                                 scalar=gate1[:, 8 + k:9 + k], in1=xT[:, k, :],
                                                 op0=ALU.mult, op1=ALU.add), xs if a else None)
            dve.wait_ge(rope_a, 3)
            then(v_.tensor_copy(cos2[:, :, 32:64], cos2[:, :, 0:32]))
            then(v_.tensor_scalar(sin2[:, :, 0:32], sin2[:, :, 32:64], -1.0, None, ALU.mult))
            norm(2)

            ss, rp = Signal(ss_done), Signal(rope_done)

            def qk(T):
                k_task, n, a = T < 2, T % 2, 44 + T
                nh = 4 if k_task else 8
                w = nh * HD
                ps = bank[a % 2][:, 0:w].rearrange("p (h d) -> p h d", d=HD)
                q_ = qw[:, T % 2, 0:w].rearrange("p (h d) -> p h d", d=HD)
                dve.wait_ge(qsq_done, T + 1)
                if k_task:
                    then(v_.tensor_copy(vt[:, n, :], bank[a % 2][:, 256:512]))
                if T >= 2:
                    dve.wait_ge(qk_tp, T - 1)
                gain = (kg if k_task else qg)[:, None, :].to_broadcast([P, nh, HD])
                ins = v_.tensor_tensor(q_, ps, gain, ALU.mult)
                ins.then_inc(acc_free[a % 2], 1)
                dve.wait_ge(acc_free[a % 2], ACC_FREE_AT[a])
                then(v_.tensor_reduce(ssq[:, T % 2, 0:nh], sqb[:, T % 2, 0:w].rearrange("p (h d) -> p h d", d=HD),
                                      AX.X, ALU.add), ss)
                dve.wait_ge(rq_done, T + 1)
                then(v_.reciprocal(ssq[:, T % 2, 0:nh], ssq[:, T % 2, 0:nh]))
                then(v_.tensor_tensor(q_, q_, ssq[:, T % 2, 0:nh][:, :, None].to_broadcast([P, nh, HD]), ALU.mult))
                r_ = rtmp[:, 0:w].rearrange("p (h d) -> p h d", d=HD)
                sn = sin2[:, n, None, :].to_broadcast([P, nh, HD])
                then(v_.tensor_tensor(r_[:, :, 0:32], q_[:, :, 32:64], sn[:, :, 0:32], ALU.mult))
                then(v_.tensor_tensor(r_[:, :, 32:64], q_[:, :, 0:32], sn[:, :, 32:64], ALU.mult))
                then(v_.tensor_tensor(q_, q_, cos2[:, n, None, :].to_broadcast([P, nh, HD]), ALU.mult))
                if k_task:
                    then(v_.tensor_tensor(kdup[:, n, :, 0, :], q_, r_, ALU.add))
                    then(v_.tensor_tensor(kdup[:, n, :, 1, :], q_, r_, ALU.add), rp)
                else:
                    then(v_.tensor_tensor(q_, q_, r_, ALU.add), rp)

            for T in range(6):
                qk(T)

            sce, nms, pns = Signal(sc_evac), Signal(nm_done), Signal(pn_done)

            def scores(h):
                dve.wait_ge(sc_mm, h + 1)
                if h >= 4:
                    dve.wait_ge(pT_mm, h - 3)
                p_ = Pb[:, h % 4, :]
                then(v_.scalar_tensor_tensor(out=p_, in0=bank[5 + h % 2][:, 0:3 * P], scalar=HD ** -0.5,
                                             in1=mask[:, :], op0=ALU.mult, op1=ALU.add), sce)
                then(v_.tensor_reduce(mx[:, h, 0:1], p_[:, 0:P], AX.X, ALU.max))
                then(v_.tensor_reduce(mx[:, h, 1:2], p_[:, P:3 * P], AX.X, ALU.max))
                then(v_.tensor_scalar(nm[:, h, :], mx[:, h, :], sinks[:, h:h + 1], -1.0, ALU.max, ALU.mult), nms)

            def probs(h):
                dve.wait_ge(exp_done, h + 1)
                then(v_.tensor_tensor(sm[:, h, :], sm[:, h, :], es[:, h, :], ALU.add))
                then(v_.reciprocal(sm[:, h, :], sm[:, h, :]))
                then(v_.tensor_scalar(Pb[:, h % 4, 0:P], Pb[:, h % 4, 0:P], sm[:, h, 0:1], None, ALU.mult))
                then(v_.tensor_scalar(Pb[:, h % 4, P:3 * P], Pb[:, h % 4, P:3 * P], sm[:, h, 1:2], None, ALU.mult), pns)

            scores(0)
            for h in range(NH):
                if h + 1 < NH:
                    scores(h + 1)
                probs(h)
                if h % 2 == 0:
                    ada(20 + h // 2)
            residual(50, 2)
            norm(3)

            R = lambda i: rt[:, i, :, 0:E]
            then(v_.memset(rt[:, 9:12, :, E:E + 1], 0.0))
            col = lambda i: rts[:, i, :]
            idx = iota[:, None, 0:E].to_broadcast([P, NB, E])
            bc = lambda i: rts[:, i, :][:, :, None].to_broadcast([P, NB, E])
            dve.wait_ge(rt_mm, 1)
            then(v_.tensor_copy(R(0), bank[5][:, 0:NB * E].rearrange("p (b e) -> p b e", b=NB)))
            for r in range(2):
                lg, oh = R(3 * r), R(3 * r + 2)
                then(v_.tensor_reduce(col(r), lg, AX.X, ALU.max))
                then(v_.tensor_tensor(R(1), lg, bc(r), ALU.is_equal))
                then(v_.scalar_tensor_tensor(out=R(1), in0=R(1), scalar=-64.0, in1=idx, op0=ALU.mult, op1=ALU.add))
                then(v_.tensor_reduce(col(2), R(1), AX.X, ALU.min))
                then(v_.tensor_tensor(oh, R(1), bc(2), ALU.is_equal))
                if r == 0:
                    then(v_.scalar_tensor_tensor(out=R(3), in0=oh, scalar=-3e38, in1=lg, op0=ALU.mult, op1=ALU.add))
            then(v_.tensor_tensor(msk, R(2), R(5), ALU.add), Signal(mask_ready))
            then(v_.tensor_tensor(col(3), col(1), col(0), ALU.subtract), Signal(rt_d))
            dve.wait_ge(rt_a, 1)
            then(v_.tensor_scalar(col(5), col(4), 1.0, None, ALU.add))
            then(v_.reciprocal(col(5), col(5)))
            then(v_.tensor_tensor(col(6), col(5), col(4), ALU.mult))
            then(v_.tensor_tensor(R(6), R(2), bc(5), ALU.mult))
            then(v_.tensor_tensor(R(7), R(5), bc(6), ALU.mult))
            then(v_.tensor_tensor(gates, R(6), R(7), ALU.add))
            dve.wait_ge(pos_mm, 1)
            then(v_.tensor_copy(pos, bank[4][:, 0:NB * E].rearrange("p (b e) -> p b e", b=NB)))
            then(v_.tensor_copy(cnt_i[:, :], bank[4][:, NB * E:NB * E + E]), Signal(cnt_ready))

            def select(g, e, blk):
                after(dve, xg_mm, g)
                for n in range(NB):
                    ins = v_.tensor_scalar(sel[:, n, :], iota[:, blk * CAP:(blk + 1) * CAP],
                                           rt[:, 10, n, bass.ds(e, 1)], rt[:, 11, n, bass.ds(e, 1)],
                                           ALU.is_equal, ALU.mult)
                ins.then_inc(sel_ready, 1)

            def rest(g):
                for i in range(2):
                    dve.wait_ge(xh_ready, g * 2 + (i + 1))
                    v_.tensor_tensor(xl[:, 4 * i:4 * i + 4, :], bank[6 + i][:, :].rearrange("p (k s) -> p k s", k=4),
                                     xh[:, 4 * i:4 * i + 4, :].bitcast(F32), ALU.subtract).then_inc(xl_ready, 1)

            def hidden_lo(j, t):
                dve.wait_ge(hh_ready, j * PAIRS + (t + 1))
                v_.tensor_tensor(hl[:, t % 2, :, :], bank[2 + t % 2][:, 0:2 * CAP].rearrange("p (i s) -> p i s", i=2),
                                 hh[:, t % 2, :, :].bitcast(F32), ALU.subtract).then_inc(hl_ready, 1)

            def job(j, e, blk=0, extra=False):
                if extra:
                    select(j + 1, e, blk)
                    rest(j + 1)
                for n, (t, part) in enumerate(step_order()):
                    dve.wait_ge(hi_ready, j * STEPS + (n + 1))
                    v_.tensor_tensor(wlo[:, n % WB, :], raw(t, part), whi[:, n % WB, :].bitcast(F32),
                                     ALU.subtract).then_inc(lo_ready, 1)
                    if (part == 1 and t) or (t == PAIRS - 1 and part == 4):
                        m = t - 1 if part == 1 else t
                        dve.wait_ge(silu_ready, j * PAIRS + (m + 1))
                        v_.tensor_tensor(hs[:, m % 2, :], silu[:, m % 2, :], bank[m % 2][:, 2 * P:4 * P],
                                         ALU.mult).then_inc(hs_ready, 1)
                    if part == 4 and t < PAIRS - 1:
                        hidden_lo(j, t)
                    if t == 1 and part == 0:
                        after(dve, selT_mm, j)
                        for b in range(NB):
                            ins = v_.tensor_scalar(selg[:, b, :], iota[:, blk * CAP:(blk + 1) * CAP],
                                                   rt[:, 10, b, bass.ds(e, 1)], rt[:, 9, b, bass.ds(e, 1)],
                                                   ALU.is_equal, ALU.mult)
                        ins.then_inc(selg_ready, 1)
                    if t == PAIRS - 3 and part == 5 and not extra:
                        select(j + 1, e + 1, 0)
                if not extra:
                    rest(j + 1)
                hidden_lo(j, PAIRS - 1)
                dve.wait_ge(step_used, j * STEPS + STEPS)
                v_.tensor_copy(y[:, 512:1024], bank[5][:, :]).then_inc(y_d, 1)
                for i in range(4):
                    dve.wait_ge(back_mm, j * 4 + (i + 1))
                    for a in range(2):
                        k = 2 * i + a
                        v_.scalar_tensor_tensor(out=xT[:, k, :], in0=bank[2 + i % 2][:, SEQ * a:SEQ * a + SEQ],
                                                scalar=gate1[:, 24 + k:25 + k], in1=xT[:, k, :],
                                                op0=ALU.mult, op1=ALU.add).then_inc(back_done, 1)
                        dve.wait_ge(back_done, j * 8 + (k + 1))

            select(0, 0, 0)
            rest(0)
            job(0, 0)
            with dve.Fori(1, E) as e:
                job(e, e)
            more_jobs(dve, job, extra=True)
            then(v_.tensor_copy(rts[:, 7, :], rts[:, 6, :]), Signal(x_final))

        @block.tensor
        def _(pe):
            mm = nc.tensor.matmul

            def transposed(dst, src, i=ident):
                return nc.tensor.transpose(dst, src, i)

            pe.wait_ge(consts, CONSTS)
            pe.wait_ge(par_in, 16 * 12)
            transposed(bank[5][:, 0:P], pa_rows[:, :], ident[:, :])
            transposed(bank[5][:, P:P + NB_ROWS], pb_rows[0:NB_ROWS, :], ident[0:NB_ROWS, 0:NB_ROWS]).then_inc(par_tp, 1)
            pe.wait_ge(x_in, 16)
            for i in range(4):
                for a in range(2):
                    for n in range(NB):
                        last = transposed(bank[(0, 1, 6, 7)[i]][:, (2 * a + n) * P:(2 * a + n + 1) * P],
                                          xin[:, n, (2 * i + a) * P:(2 * i + a + 1) * P], ident[:, :])
                last.then_inc(x_tp, 1)

            def arrived(name):
                s, at = full_at[name_of[name]]
                pe.wait_ge(ring_full[s], at)
                return ring[s]

            def columns(name):
                return arrived(name)[:, 0:KC * UC].rearrange("p (k n) -> p k n", k=KC)

            tasks = [0]

            def acc_bank():
                T = tasks[0]
                tasks[0] += 1
                if T >= 2:
                    wait_free(pe, T - 2)
                return T, bank[T % 2]

            def stats(q):
                for k in range(KC):
                    if k % 2 == 0:
                        pe.wait_ge(sq_done, 4 * q + k // 2 + 1)
                    last = mm(bank[4][:, 0:SEQ], mean_w[:, :], B[:, k, :], start=k == 0, stop=k == KC - 1)
                last.then_inc(stat_mm, 1)

            def ada(v):
                w = columns(("ada", v))
                if v >= 2:
                    pe.wait_ge(ada_done, v - 1)
                for i in range(4):
                    for k in range(KC):
                        last = mm(bank[2 + v % 2][:, i:i + 1], w[:, k, i * P:(i + 1) * P], cact[:, k:k + 1],
                                  start=k == 0, stop=k == KC - 1)
                last.then_inc(ada_mm, 1)


            def project(name, src, h0=None):
                w = columns(name)
                for tk in range(2):
                    T, b = acc_bank()
                    for a in range(2):
                        i = 2 * tk + a
                        for k in range(KC):
                            if h0 is not None and tk == 0 and a == 0:
                                pe.wait_ge(h_done, h0 + k + 1)
                            last = mm(b[:, SEQ * a:SEQ * a + SEQ], w[:, k, i * P:(i + 1) * P], src[:, k, :],
                                      start=k == 0, stop=k == KC - 1)
                    last.then_inc(acc_full[T % 2], 1)

            stats(0)
            pe.wait_ge(cact_ready, 1)
            for v in range(4):
                ada(v)
            for i in range(4):
                project(("in", i), H, 0 if i == 0 else None)
            w = arrived("gates")
            for k in range(KC):
                T, b = acc_bank()
                if k % 2 == 0:
                    pe.wait_ge(conv_done, k // 2 + 1)
                else:
                    wait_free(pe, k // 2)
                mm(b[:, 0:SEQ], w[:, k * P:(k + 1) * P], C[:, k, :], start=True, stop=True)
                mm(b[:, SEQ:2 * SEQ], w[:, 1024 + k * P:1024 + (k + 1) * P], C[:, k, :], start=True,
                   stop=True).then_inc(acc_full[T % 2], 1)
            for v in range(4, 10):
                ada(v)
            pe.wait_ge(mix_done, KC)
            for i in range(2):
                project(("out", i), C)
            stats(1)

            def gate_up(w, srcs, bank_of, width, free, done):
                for i in range(2):
                    b = bank_of(i)
                    free(i)
                    for half, off in ((0, 0), (1, SEQ)):
                        wv = w[:, 2048 * half:2048 * half + 2048].rearrange("p (k n) -> p k n", k=KC)
                        for k in range(KC):
                            last = mm(b[:, off:off + width], wv[:, k, i * P:(i + 1) * P], srcs[:, k, 0:width],
                                      start=k == 0, stop=k == KC - 1)
                    done(i, last)

            def dense_down(t):
                s = full_at[name_of[("ff", t)]][0]
                for i in range(2):
                    pe.wait_ge(hid_done, 2 * t + i + 1)
                    wv = ring[s][:, 4096 + 1024 * i:4096 + 1024 * (i + 1)]
                    for k in range(KC):
                        last = mm(bank[4 + k // 2][:, SEQ * (k % 2):SEQ * (k % 2) + SEQ], wv[:, k * P:(k + 1) * P],
                                  hid[:, t % 2, i, :], start=t == 0 and i == 0 and k % 2 == 0,
                                  stop=t == PAIRS_DENSE - 1 and i == 1, skip_group_check=True)
                last.then_inc(down_mm, 1)

            pe.wait_ge(h_done, 16)
            for t in range(PAIRS_DENSE):
                s, at = full_at[name_of[("ff", t)]]
                pe.wait_ge(ring_full[s], at)

                gate_up(ring[s], H, lambda i: bank[i], SEQ, lambda i: acc_bank(),
                        lambda i, last: last.then_inc(acc_full[i], 1))
                if t:
                    dense_down(t - 1)
                    if t - 1 < 10:
                        ada(10 + t - 1)
            dense_down(PAIRS_DENSE - 1)

            stats(2)
            w_kv_ = columns("kv")
            for n in range(NB):
                T, b = acc_bank()
                for k in range(KC):
                    if n == 0:
                        pe.wait_ge(h_done, 16 + k + 1)
                    last = mm(b[:, :], H[:, k, n * P:(n + 1) * P], w_kv_[:, k, :], start=k == 0, stop=k == KC - 1)
                last.then_inc(acc_full[T % 2], 1)

            def to_T(T):
                pe.wait_ge(rope_done, T + 1)
                if T >= 2:
                    pe.wait_ge(qkT_done, T - 1)
                for i in range(4):
                    src = (kdup[:, T, :, :, :].rearrange("p h t d -> p (h t d)") if T < 2 else qw[:, T % 2, :])
                    last = transposed(bank[5 + T % 2][:, i * P:(i + 1) * P], src[:, i * P:(i + 1) * P], ident[:, :])
                last.then_inc(qk_tp, 1)

            pe.wait_ge(h_done, 32)
            for hf in range(2):
                wq = columns(("q", hf))
                for n in range(NB):
                    T, b = acc_bank()
                    for k in range(KC):
                        last = mm(b[:, :], C[:, k, n * P:(n + 1) * P], wq[:, k, :], start=k == 0, stop=k == KC - 1)
                    last.then_inc(acc_full[T % 2], 1)
                    to_T(2 * hf + n)
            to_T(4)
            to_T(5)

            def scores(h):
                lo, k, g = HD * (h % 2), h // 2, h // (NH // NKV)
                if h >= 2:
                    pe.wait_ge(sc_evac, h - 1)
                else:
                    pe.wait_ge(qkT_done, 6)
                q_ = B[lo:lo + HD, k, :]
                mm(bank[5 + h % 2][:, 0:P], q_[:, 0:P], kT[lo:lo + HD, g, 0:P], start=True, stop=True)
                mm(bank[5 + h % 2][:, P:3 * P], q_[:, P:2 * P], kT[lo:lo + HD, g, :], start=True,
                   stop=True).then_inc(sc_mm, 1)

            def probs_T(h):
                pe.wait_ge(pn_done, h + 1)
                if h >= 2:
                    pe.wait_ge(pT_evac, h - 1)
                b = bank[7 if h % 2 else 4]
                for i in range(3):
                    last = transposed(b[:, i * P:(i + 1) * P], Pb[:, h % 4, i * P:(i + 1) * P], ident[:, :])
                last.then_inc(pT_mm, 1)

            def values(h):
                lo, k, g = HD * (h % 2), h // 2, h // (NH // NKV)
                pe.wait_ge(pT_evac, h + 1)
                if h % 2 == 0 and k >= 2:
                    pe.wait_ge(o_evac, k - 1)
                o = bank[k % 2][lo:lo + HD, :]
                v0, v1 = vt[:, 0, g * HD:(g + 1) * HD], vt[:, 1, g * HD:(g + 1) * HD]
                p_ = PT[:, h % 2, :]
                mm(o[:, 0:P], v0, p_[:, 0:P], start=True, stop=True)
                mm(o[:, P:2 * P], v0, p_[:, P:2 * P], start=True, stop=False)
                mm(o[:, P:2 * P], v1, p_[:, 2 * P:3 * P], start=False, stop=True).then_inc(pv_mm, 1)

            for h in range(3):
                scores(h)
            for h in range(NH):
                probs_T(h)
                if h:
                    values(h - 1)
                if h + 3 < NH:
                    scores(h + 3)
                if h % 2 == 0:
                    ada(20 + h // 2)
            values(NH - 1)
            pe.wait_ge(o_evac, KC)
            for i in range(2):
                project(("o", i), A)
            assert tasks[0] == acc_tasks
            stats(3)

            for n in range(NB):
                for k in range(KC):
                    if n == 0:
                        pe.wait_ge(h_done, 32 + k + 1)
                    last = mm(bank[5][:, n * E:(n + 1) * E], H[:, k, n * P:(n + 1) * P], rt_w[:, k, :],
                              start=k == 0, stop=k == KC - 1)
            last.then_inc(rt_mm, 1)
            for i in range(4):
                if i >= 2:
                    pe.wait_ge(ht_done, i - 1)
                for a in range(4):
                    last = transposed(bank[6 + i % 2][:, a * P:(a + 1) * P],
                                      H[:, 4 * (i % 2) + a, (i // 2) * P:(i // 2 + 1) * P], ident[:, :])
                last.then_inc(ht_tp, 1)
            pe.wait_ge(mask_ready, 1)
            mm(bank[4][:, 0:E], before[:, :], msk[:, 0, :], start=True, stop=True)
            mm(bank[4][:, E:2 * E], before[:, :], msk[:, 1, :], start=True, stop=False)
            mm(bank[4][:, E:2 * E], ones[:, :], msk[:, 0, :], start=False, stop=True)
            mm(bank[4][:, 2 * E:3 * E], ones[:, :], msk[:, 0, :], start=True, stop=False)
            mm(bank[4][:, 2 * E:3 * E], ones[:, :], msk[:, 1, :], start=False, stop=True).then_inc(pos_mm, 1)
            for T in (acc_tasks - 2, acc_tasks - 1):
                wait_free(pe, T)
            pe.wait_ge(ht_done, 4)
            pe.wait_ge(cnt_ready, 1)

            def gather(g):
                pe.wait_ge(sel_ready, g + 1)
                after(pe, xl_ready, g * 2)
                for k in range(KC):
                    for n in range(NB):
                        last = mm(bank[6 + k // 4][:, (k % 4) * CAP:(k % 4 + 1) * CAP], htok[:, n, k * P:(k + 1) * P],
                                  sel[:, n, :], start=n == 0, stop=n == NB - 1)
                last.then_inc(xg_mm, 1)

            def split_product(o, hi, lo, w, start, stop):
                b, c0 = w
                mm(o, hi, whi[:, b, c0:c0 + 512], start=start, stop=False)
                mm(o, lo, whi[:, b, c0:c0 + 512], start=False, stop=False)
                return mm(o, hi, wlo[:, b, c0:c0 + 512], start=False, stop=stop)

            def hidden_T(j, t):
                pe.wait_ge(hs_ready, j * PAIRS + (t + 1))
                if t == 0:
                    after(pe, back_done, j * 8)
                elif t == 1:
                    pe.wait_ge(selT_ready, j + 1)
                after(pe, hl_ready, j * PAIRS + max(0, t - 1))
                for i in range(2):
                    last = transposed(bank[2 + t % 2][:, i * P:(i + 1) * P], hs[:, t % 2, i * P:(i + 1) * P], ident[:, :])
                last.then_inc(hT_mm, 1)

            def job(j, e, blk=0, extra=False):
                g = j + 1 if extra else j
                if extra:
                    gather(g)
                pe.wait_ge(xl_ready, g * 2 + 2)
                for n, (t, part) in enumerate(step_order()):
                    if part == 0:
                        after(pe, hs_ready, j * PAIRS + max(0, t - 1))
                    if part == 4:
                        pe.wait_ge(hl_ready, j * PAIRS + (t + 1))
                    pe.wait_ge(lo_ready, j * STEPS + (n + 1))
                    for a in range(2):
                        w = (n % WB, 512 * a)
                        if part < 4:
                            k = 2 * part + a
                            last = split_product(bank[t % 2][:, :], xh[:, k, :], xl[:, k, :], w, k == 0, k == KC - 1)
                        else:
                            i = part - 4
                            last = split_product(bank[4 + a][:, :], hh[:, t % 2, i, :], hl[:, t % 2, i, :], w,
                                                 t == 0 and i == 0, t == PAIRS - 1 and i == 1)
                    last.then_inc(step_used, 1)
                    if part == 1 and t:
                        hidden_T(j, t - 1)
                    if t == PAIRS - 2 and part == 4:
                        hidden_T(j, PAIRS - 1)
                    if t == 0 and part == 4:
                        pe.wait_ge(selg_ready, j + 1)
                        after(pe, hl_ready, j * PAIRS)
                        for b in range(NB):
                            last = transposed(bank[3][:, b * P:(b + 1) * P], selg[:, b, :], ident[:, :])
                        last.then_inc(selT_mm, 1)
                    if t == PAIRS - 1 and part == 3 and not extra:
                        gather(j + 1)
                pe.wait_ge(y_a, j + 1)
                pe.wait_ge(y_d, j + 1)
                pe.wait_ge(selT_ready, j + 1)
                for i in range(4):
                    after(pe, back_done, j * 8 + max(0, 2 * (i - 1)))
                    for a in range(2):
                        k = 2 * i + a
                        last = mm(bank[2 + i % 2][:, SEQ * a:SEQ * a + SEQ], y[:, k * P:(k + 1) * P], selT[:, :],
                                  start=True, stop=True)
                    last.then_inc(back_mm, 1)

            gather(0)
            job(0, 0)
            with pe.Fori(1, E) as e:
                job(e, e)
            more_jobs(pe, job, extra=True)
            pe.wait_ge(x_final, 1)
            for i in range(4):
                if i >= 2:
                    pe.wait_ge(fin_evac, i - 1)
                for a in range(4):
                    last = transposed(bank[6 + i % 2][:, a * P:(a + 1) * P],
                                      xT[:, 4 * (i % 2) + a, (i // 2) * P:(i // 2 + 1) * P], ident[:, :])
                last.then_inc(fin_tp, 1)


NAMES = ["x", "c", "positions", "inv_freq", "ada_w", "ada_b", "mix_norm", "ffn_norm", "a_w_in", "a_conv_w", "a_conv_b",
         "a_gx_w", "a_gx_b", "a_ga_w", "a_ga_b", "a_lambda", "a_w_out", "kv_norm", "kv_ada_w", "kv_ada_b", "w_kv",
         "k_norm", "b_w_q", "b_q_norm", "b_sinks", "b_w_o", "f_w_gu", "f_w_down", "m_router", "m_w_gu", "m_w_down"]


def kernel(**inputs):
    import numpy as np
    import concourse.bacc as bacc
    from concourse.bass_utils import run_bass_kernel_spmd

    inv = (np.float32(10000.0) ** (-np.arange(0, HD, 2, dtype=np.float32) / np.float32(HD))).astype(np.float32)
    nc = bacc.Bacc("TRN2", target_bir_lowering=False, num_devices=1)
    arrays, args = {}, []
    for name in NAMES:
        a = np.ascontiguousarray(inv[None, :] if name == "inv_freq" else inputs[name])
        arrays[f"in_{name}"] = a
        args.append(nc.dram_tensor(f"in_{name}", a.shape, mybir.dt.from_np(a.dtype), kind="ExternalInput").ap())
    args.append(nc.dram_tensor("out_0", (1, SEQ, D), F32, kind="ExternalOutput").ap())
    build(nc, *args)
    r = run_bass_kernel_spmd(nc, [arrays], core_ids=[0])
    return r.results[0]["out_0"]
```

```python
import math
from contextlib import ExitStack

import concourse.bass as bass
from concourse import mybir

F32 = mybir.dt.float32
I32 = mybir.dt.int32
F32R = mybir.dt.float32r
ALU = mybir.AluOpType
ACT = mybir.ActivationFunctionType
AX = mybir.AxisListType

P = 128
D = 1024
SEQ = 256
KC = D // P
NB = SEQ // P
D_FF = 3 * D
FE = 7 * D // 2
E = 8
HD = 64
NH = D // HD
NKV = 4
EPS = 1e-6
LRU_C = 8.0
CAP = 128
NBLK = -(-SEQ // CAP)
RING = 7
WB = 4
SLOT = 4096
UC = 512
PAIRS_DENSE = D_FF // (2 * P)
PAIRS = FE // (2 * P)
UNITS = 3 * PAIRS // 2
STEPS = 6 * PAIRS
NEG = -1e30
TWO_PI = (6.28125, 0.0019350051879882812, 3.019916050561733e-07)


class Signal:

    def __init__(self, sem):
        self.sem, self.n = sem, 0

    def up(self, ins):
        ins.then_inc(self.sem, 1)
        self.n += 1


def build(nc, x, c, positions, inv_freq, ada_w, ada_b, mix_norm, ffn_norm, a_w_in, a_conv_w, a_conv_b,
          a_gx_w, a_gx_b, a_ga_w, a_ga_b, a_lambda, a_w_out, kv_norm, kv_ada_w, kv_ada_b, w_kv,
          k_norm, b_w_q, b_q_norm, b_sinks, b_w_o, f_w_gu, f_w_down, m_router, m_w_gu, m_w_down, out):
    ctx = ExitStack()
    with ctx:
        def sb(name, shape, dt=F32):
            return ctx.enter_context(nc.sbuf_tensor(name, shape, dt))

        def sem(name):
            return ctx.enter_context(nc.semaphore(name))

        ring = [sb(f"ring{i}", [P, SLOT]) for i in range(RING)]
        xT = sb("xT", [P, KC, SEQ])
        A = sb("A", [P, KC, SEQ])
        cols = sb("cols", [P, 224])
        mod = sb("mod", [P, 112])
        aff = sb("aff", [P, 40])
        gate1 = sb("gate1", [P, 32])
        cact = sb("cact", [P, 8])
        lru = sb("lru", [P, 8, 8])
        s8 = lru[:, 7, :]
        eps = sb("eps", [P, 1])
        ident = sb("ident", [P, P])
        ones = sb("ones", [P, P])
        mean_w = sb("mean_w", [P, P])
        before = sb("before", [P, P])
        mask = sb("mask", [P, 3 * P])
        iota = sb("iota", [P, NBLK * CAP])
        rms = sb("rms", [P, SEQ])
        rstd = sb("rstd", [P, SEQ])
        silu = sb("silu", [P, 2, SEQ])
        lt = silu
        pos_i = sb("pos_i", [P, NB], I32)
        ang = sb("ang", [P, NB, HD // 2])
        turn = sb("turn", [P, NB, HD // 2])
        turn_i = sb("turn_i", [P, NB, HD // 2], I32)
        posf = sb("posf", [P, NB])
        inv_bc = sb("inv_bc", [P, HD // 2])
        cos2 = sb("cos2", [P, NB, HD])
        sin2 = sb("sin2", [P, NB, HD])
        kg = sb("kg", [P, HD])
        qg = sb("qg", [P, HD])
        sinks = sb("sinks", [P, NH])
        half_pi = sb("half_pi", [P, 1])
        ssq = sb("ssq", [P, 2, 8])
        mx = sb("mx", [P, NH, 2])
        nm = sb("nm", [P, NH, 2])
        sm = sb("sm", [P, NH, 2])
        es = sb("es", [P, NH, 2])
        rt_w = sb("rt_w", [P, KC, E])
        rt = sb("rt", [P, 12, NB, E + 1])
        rts = sb("rts", [P, 8, NB])
        cnt_i = sb("cnt_i", [P, E + 1], I32)
        bank = [ctx.enter_context(nc.psum_tensor(f"bank{i}", [P, 512], F32)) for i in range(8)]

        with ExitStack() as region:
            def shared(name, shape, dt=F32):
                return region.enter_context(nc.sbuf_tensor(name, shape, dt))

            H = shared("H", [P, KC, SEQ])
            G = shared("G", [P, KC, SEQ])
            B = shared("B", [P, KC, SEQ])
            C = shared("C", [P, KC, SEQ])
            Dd = shared("Dd", [P, KC, SEQ])
            dup = shared("dup", [P, 1024])
            PT = shared("PT", [P, 2, 512])
            rtmp = shared("rtmp", [P, UC])
            kT = shared("kT", [P, NKV, SEQ])
            vt = shared("vt", [P, NB, NKV * HD])
            sqb = shared("sqb", [P, 2, UC])
            qw = shared("qw", [P, 2, UC])
        with ExitStack() as region:
            fh = shared("fh", [P, KC, SEQ], F32R)
            dhi = shared("dhi", [P, WB, 1024], F32R)
            dlo = shared("dlo", [P, WB, 1024], F32R)
            gh = shared("gh", [P, 2, 2, SEQ], F32R)
            gl = shared("gl", [P, 2, 2, SEQ], F32R)
            fl = shared("fl", [P, KC, SEQ], F32R)
        with ExitStack() as region:
            whi = shared("whi", [P, WB, 1024], F32R)
            wlo = shared("wlo", [P, WB, 1024], F32R)
            xh = shared("xh", [P, KC, CAP], F32R)
            xl = shared("xl", [P, KC, CAP], F32R)
            hs = shared("hs", [P, 2, 2 * P])
            hh = shared("hh", [P, 2, 2, CAP], F32R)
            hl = shared("hl", [P, 2, 2, CAP], F32R)
            y = shared("y", [CAP, D])
            sel = shared("sel", [P, NB, CAP])
            selg = shared("selg", [P, NB, CAP])
            selT = shared("selT", [CAP, SEQ])
        ada_acc = lambda v: (sqb if v % 4 < 2 else qw)[:, v % 2, :]
        iota_i = rtmp[:, 0:NBLK * CAP].bitcast(I32)
        kdup = dup[:, :].rearrange("p (b h t d) -> p b h t d", b=NB, h=NKV, t=2)
        pa_rows, pb_rows = B[:, 0, 0:P], B[:, 0, P:2 * P]
        Pb = Dd[:, :, :].rearrange("p k n -> p (k n)")[:, 0:4 * 3 * P].rearrange("p (b n) -> p b n", b=4)
        htok = A[:, :, :].rearrange("p k n -> p (k n)").rearrange("p (b n) -> p b n", b=NB)
        xin = Dd[:, :, :].rearrange("p k n -> p (k n)").rearrange("p (b n) -> p b n", b=NB)
        otok = A[:, :, :].rearrange("p k n -> p (k n)").rearrange("p (b n) -> p b n", b=NB)
        gates, pos, msk = rt[:, 9, :, 0:E], rt[:, 10, :, 0:E], rt[:, 11, :, 0:E]

        CA_BIAS, CA_MIX = 0, 112
        CB = P
        CB_FFN, CB_KVN, CB_CONVW, CB_CONVB, CB_GXB, CB_GAB, CB_LAM, CB_C = (
            CB, CB + 16, CB + 24, CB + 56, CB + 64, CB + 72, CB + 80, CB + 88)
        NB_ROWS = 96

        par_in = sem("par_in")
        x_in = sem("x_in")
        misc_in = sem("misc_in")
        ring_full = [sem(f"ring_full{i}") for i in range(RING)]
        out_stored = sem("out_stored")
        consts = sem("consts")
        par_tp = sem("par_tp")
        cols_ready = sem("cols_ready")
        x_tp = sem("x_tp")
        acc_full = [sem(f"acc_full{b}") for b in range(2)]
        acc_free = [sem(f"acc_free{b}") for b in range(2)]
        ada_sum = sem("ada_sum")
        ada_mm = sem("ada_mm")
        ada_done = sem("ada_done")
        cact_ready = sem("cact_ready")
        mod_ready = sem("mod_ready")
        dve_step = sem("dve_step")
        act_step = sem("act_step")
        x_new = sem("x_new")
        sq_done = sem("sq_done")
        stat_mm = sem("stat_mm")
        rms_done = sem("rms_done")
        xn_done = sem("xn_done")
        h_done = sem("h_done")
        conv_done = sem("conv_done")
        lam_a = sem("lam_a")
        lam_d = sem("lam_d")
        lru_a = sem("lru_a")
        lru_var = sem("lru_var")
        lru_beta = sem("lru_beta")
        mix_done = sem("mix_done")
        fx_ready = sem("fx_ready")
        fh_ready = sem("fh_ready")
        fl_ready = sem("fl_ready")
        dhi_ready = sem("dhi_ready")
        dlo_ready = sem("dlo_ready")
        dense_used = sem("dense_used")
        silu_done = sem("silu_done")
        hid_done = sem("hid_done")
        gh_ready = sem("gh_ready")
        gl_ready = sem("gl_ready")
        rope_a = sem("rope_a")
        rope_d = sem("rope_d")
        qsq_done = sem("qsq_done")
        ss_done = sem("ss_done")
        rq_done = sem("rq_done")
        rope_done = sem("rope_done")
        qk_tp = sem("qk_tp")
        qkT_done = sem("qkT_done")
        sc_mm = sem("sc_mm")
        sc_evac = sem("sc_evac")
        nm_done = sem("nm_done")
        exp_done = sem("exp_done")
        pn_done = sem("pn_done")
        pT_mm = sem("pT_mm")
        pT_evac = sem("pT_evac")
        pv_mm = sem("pv_mm")
        o_evac = sem("o_evac")
        rt_mm = sem("rt_mm")
        mask_ready = sem("mask_ready")
        pos_mm = sem("pos_mm")
        cnt_ready = sem("cnt_ready")
        rt_a = sem("rt_a")
        rt_d = sem("rt_d")
        ht_tp = sem("ht_tp")
        ht_done = sem("ht_done")
        sel_ready = sem("sel_ready")
        xg_mm = sem("xg_mm")
        xh_ready = sem("xh_ready")
        xl_ready = sem("xl_ready")
        selg_ready = sem("selg_ready")
        selT_mm = sem("selT_mm")
        selT_ready = sem("selT_ready")
        hi_ready = sem("hi_ready")
        lo_ready = sem("lo_ready")
        step_used = sem("step_used")
        silu_ready = sem("silu_ready")
        hs_ready = sem("hs_ready")
        hT_mm = sem("hT_mm")
        hh_ready = sem("hh_ready")
        hl_ready = sem("hl_ready")
        y_a = sem("y_a")
        y_d = sem("y_d")
        back_mm = sem("back_mm")
        back_done = sem("back_done")
        x_final = sem("x_final")
        fin_tp = sem("fin_tp")
        fin_evac = sem("fin_evac")

        def cols_of(w, c0):
            src = w.rearrange("(k p) n -> p k n", p=P)[:, :, c0:c0 + UC]
            return [(lambda s: s[:, 0:KC * UC].rearrange("p (k n) -> p k n", k=KC), src)]

        def gate_up_of(gu, ff, t):
            f0 = 2 * P * t
            g = gu.rearrange("(k p) n -> p k n", p=P)
            side = lambda s: s[:, :].rearrange("p (k h n) -> p k h n", k=KC, h=2)
            return [(lambda s: side(s)[:, :, 0, :], g[:, :, f0:f0 + 2 * P]),
                    (lambda s: side(s)[:, :, 1, :], g[:, :, ff + f0:ff + f0 + 2 * P])]

        def down_of(down, m):
            return [(lambda s: s[:, :].rearrange("p (i n) -> p i n", i=4),
                     down[4 * P * m:4 * P * (m + 1), :].rearrange("(i p) n -> p i n", p=P))]

        units, name_of, last_use = [], {}, []

        def unit(name, parts, used_by):
            name_of[name] = len(units)
            units.append(parts)
            last_use.append(used_by)

        def task_end(T):
            return acc_full[T % 2], ACC_FULL_AT[T]

        ACC_FULL_AT = {T: T // 2 + 1 for T in range(30)}

        ADA_IN_DENSE = 15

        ADA_ON_PE = 1

        def ada_sum_at(v):
            return v + 1 if v < ADA_ON_PE else v

        def step_order(pairs=PAIRS):
            for t in range(pairs + 1):
                for part in range(4 if t < pairs else 0):
                    yield t, part
                for part in range(4, 6 if t else 4):
                    yield t - 1, part

        dense_steps = list(step_order(PAIRS_DENSE))
        DSTEPS = len(dense_steps)

        def ada_ops_beside(n):
            ops = KC * ADA_IN_DENSE
            return [(10 + m // KC, m % KC) for m in range(ops * n // DSTEPS, ops * (n + 1) // DSTEPS)]

        def ada_summed_by(t):
            return [v for n, (p, _) in enumerate(dense_steps) for v, k in ada_ops_beside(n)
                    if k == KC - 1 and dense_pair_time(n) == t]

        def dense_pair_time(n):
            return next((dense_steps[m][0] for m in range(n + 1, DSTEPS) if dense_steps[m][1] == 0), PAIRS_DENSE)

        def ada_beside(t):
            n = ADA_IN_DENSE
            return range(10 + n * t // PAIRS_DENSE, 10 + n * (t + 1) // PAIRS_DENSE)

        def ada_unit(v):
            w, v0 = (ada_w[0], 0) if v < 12 else (kv_ada_w, 12) if v < 16 else (ada_w[1], 16)
            unit(("ada", v), cols_of(w, (v - v0) * UC), (ada_mm, v + 1) if v == ADA_ON_PE else (ada_sum, ada_sum_at(v)))

        for v in range(4):
            ada_unit(v)
        for i in range(3):
            unit(("in", i), cols_of(a_w_in[0], i * UC), task_end(2 * i + 1))
        unit("gates", [
            (lambda s: s[:, 0:1024].rearrange("p (k n) -> p k n", k=8), a_ga_w[0].rearrange("b c d -> c b d")),
            (lambda s: s[:, 1024:2048].rearrange("p (k n) -> p k n", k=8), a_gx_w[0].rearrange("b c d -> c b d"))],
            task_end(13))
        for v in range(4, 6):
            ada_unit(v)
        unit(("in", 3), cols_of(a_w_in[0], 3 * UC), task_end(15))
        for i in range(2):
            unit(("out", i), cols_of(a_w_out[0], i * UC), task_end(17 + 2 * i))
        for v in range(6, 10):
            ada_unit(v)
        for t in range(PAIRS_DENSE):
            unit(("gu", t), gate_up_of(f_w_gu[0], D_FF, t), (dlo_ready, dense_steps.index((t, 3)) + 1))
            if t % 2:
                unit(("down", t // 2), down_of(f_w_down[0], t // 2), (dlo_ready, dense_steps.index((t, 5)) + 1))
            for v in ada_beside(t):
                ada_unit(v)
        unit("kv", cols_of(w_kv, 0), task_end(21))
        ada_unit(25)
        for i in range(2):
            unit(("q", i), cols_of(b_w_q[0], i * UC), task_end(23 + 2 * i))
        for v in (26, 27):
            ada_unit(v)
        for i in range(2):
            unit(("o", i), cols_of(b_w_o[0], i * UC), task_end(27 + 2 * i))
        U0 = len(units)
        full_at, sofar = [], [0] * RING
        for u in range(U0):
            s = (u - U0) % RING
            sofar[s] += 16 * len(units[u])
            full_at.append((s, sofar[s]))

        def unit_of(t, part):
            return 3 * (t // 2) + (t % 2 if part < 4 else 2)

        assert UNITS % RING == 0
        transfers = [1 if i % 3 == 2 else 2 for i in range(UNITS)]
        per_job = [16 * sum(transfers[i] for i in range(s, UNITS, RING)) for s in range(RING)]
        landed_at = [sofar[i % RING] + 16 * sum(transfers[n] for n in range(i % RING, i + 1, RING)) for i in range(UNITS)]
        last_step = {unit_of(t, part): n + 1 for n, (t, part) in enumerate(step_order())}
        freed_at = [last_step[i - RING] if i >= RING else last_step[i - RING + UNITS] - STEPS for i in range(UNITS)]

        acc_tasks = 30

        ACC_FREE_AT = {T: T // 2 + 1 for T in range(16)} | {T: 9 + (T - 20) // 2 for T in range(20, 26)}

        def after(eng, sem, v):
            if not isinstance(v, int) or v > 0:
                eng.wait_ge(sem, v)

        def wait_free(eng, T):
            if 16 <= T < 20:
                eng.wait_ge(x_new, 4 + T - 16 + 1)
            elif T >= 26:
                eng.wait_ge(x_new, 12 + T - 26 + 1)
            else:
                eng.wait_ge(acc_free[T % 2], ACC_FREE_AT[T])

        def more_jobs(eng, job, **how):
            reg = eng.alloc_register(f"job_{eng.engine.name}")
            eng.reg_mov(reg, E)
            most = eng.value_load(cnt_i[0:1, E:E + 1], min_val=0, max_val=SEQ)
            with eng.If(most > CAP):
                with eng.Fori(0, E) as e:
                    n = eng.value_load(cnt_i[0:1, bass.ds(e, 1)], min_val=0, max_val=SEQ)
                    for b in range(1, NBLK):
                        with eng.If(n > b * CAP):
                            j = eng.snap(reg, min_val=E, max_val=E * NBLK)
                            job(j, e, b, **how)
                            eng.reg_add(reg, reg, 1)

        def dense_raw(t, part):
            row = part if part < 4 else 2 * (t % 2) + part - 4
            s = full_at[name_of[("gu", t) if part < 4 else ("down", t // 2)]][0]
            return ring[s][:, 1024 * row:1024 * (row + 1)]

        def raw(t, part):
            row = part if part < 4 else 2 * (t % 2) + part - 4
            return ring[unit_of(t, part) % RING][:, 1024 * row:1024 * (row + 1)]

        CONSTS = 12

        rows = [(pb_rows, 88, c[0]),
                (pa_rows, 0, ada_b[0]), (pa_rows, 48, kv_ada_b), (pa_rows, 64, ada_b[1]),
                (pa_rows, 112, mix_norm.rearrange("l n -> (l n)")), (pb_rows, 0, ffn_norm.rearrange("l n -> (l n)")),
                (pb_rows, 16, kv_norm), (pb_rows, 24, a_conv_w[0].rearrange("l n -> (l n)")),
                (pb_rows, 56, a_conv_b[0]), (pb_rows, 64, a_gx_b[0]), (pb_rows, 72, a_ga_b[0]),
                (pb_rows, 80, a_lambda[0])]
        ROWS_ON_SP = 5

        block = ctx.enter_context(nc.Block())

        @block.sync
        def _(sp):
            sp.dma_start(xin[:, 0:NB, :], x[0].rearrange("(b p) n -> p b n", p=P)).then_inc(x_in, 16)
            for dst, r, src in rows[:ROWS_ON_SP]:
                v = src.rearrange("(r n) -> r n", n=P)
                sp.dma_start(dst[r:r + v.shape[0], :], v).then_inc(par_in, 16)
            for u, parts in enumerate(units):
                s = full_at[u][0]
                if u >= RING:
                    sp.wait_ge(*last_use[u - RING])
                for dst, src in parts:
                    sp.dma_start(dst(ring[s]), src).then_inc(ring_full[s], 16)

            def job(j, e, blk=0):
                gu = m_w_gu[0][bass.ds(e, 1)].rearrange("o r n -> (o r) n")
                down = m_w_down[0][bass.ds(e, 1)].rearrange("o r n -> (o r) n")
                for i in range(UNITS):
                    if isinstance(j, int) and i < RING:
                        sp.wait_ge(*last_use[U0 + i - RING])
                    else:
                        sp.wait_ge(lo_ready, j * STEPS + freed_at[i])
                    parts = down_of(down, i // 3) if i % 3 == 2 else gate_up_of(gu, FE, 2 * (i // 3) + i % 3)
                    for dst, src in parts:
                        sp.dma_start(dst(ring[i % RING]), src).then_inc(ring_full[i % RING], 16)

            job(0, 0)
            with sp.Fori(1, E) as e:
                job(e, e)
            sp.wait_ge(cnt_ready, 1)
            more_jobs(sp, job)
            for n in range(NB):
                sp.wait_ge(fin_evac, 2 * n + 2)
                sp.dma_start(out[0][n * P:(n + 1) * P, :], otok[:, n, :]).then_inc(out_stored, 16)
            sp.wait_ge(out_stored, 16 * NB)

        @block.gpsimd
        def _(pool):
            made = Signal(consts)

            def do(ins):
                made.up(ins)
                pool.wait_ge(consts, made.n)

            do(nc.gpsimd.memset(eps[:, :], EPS))
            do(nc.gpsimd.memset(half_pi[:, :], math.pi / 2))
            do(nc.gpsimd.memset(ones[:, :], 1.0))
            do(nc.gpsimd.memset(mean_w[:, :], 1.0 / D))
            do(nc.gpsimd.affine_select(out=ident[:, :], in_=ones[:, :], compare_op=ALU.is_equal, fill=0.0, base=0,
                                       pattern=[[-1, P]], channel_multiplier=1))
            do(nc.gpsimd.affine_select(out=before[:, :], in_=ones[:, :], compare_op=ALU.is_gt, fill=0.0, base=0,
                                       pattern=[[1, P]], channel_multiplier=-1))
            do(nc.gpsimd.memset(mask[:, :], 0.0))
            for i, (sign, op) in enumerate(((1, ALU.is_ge), (-1, ALU.is_gt), (1, ALU.is_ge))):
                m = mask[:, i * P:(i + 1) * P]
                do(nc.gpsimd.affine_select(out=m, in_=m, compare_op=op, fill=NEG, base=0,
                                           pattern=[[-sign, P]], channel_multiplier=sign))
            do(nc.gpsimd.iota(iota_i[:, :], pattern=[[1, NBLK * CAP]], base=0, channel_multiplier=0))
            do(nc.gpsimd.tensor_copy(iota[:, :], iota_i[:, :]))
            assert made.n == CONSTS

        @block.scalar
        def _(act):
            step = Signal(act_step)

            def then(ins, signal=None):
                s = signal or step
                s.up(ins)
                act.wait_ge(s.sem, s.n)

            for dst, r, src in rows[ROWS_ON_SP:]:
                v = src.rearrange("(r n) -> r n", n=P)
                act.dma_start(dst[r:r + v.shape[0], :], v).then_inc(par_in, 16)
            with nc.allow_non_contiguous_dma(reason="256 positions, one per partition"):
                act.dma_start(pos_i[:, :], positions[0].rearrange("(b p) -> p b", p=P)).then_inc(misc_in, 16)
            act.dma_start(inv_bc[:, :], inv_freq.to_broadcast([P, HD // 2])).then_inc(misc_in, 16)
            act.dma_start(kg[:, :], k_norm[None, :].to_broadcast([P, HD])).then_inc(misc_in, 16)
            act.dma_start(qg[:, :], b_q_norm.to_broadcast([P, HD])).then_inc(misc_in, 16)
            act.dma_start(sinks[:, :], b_sinks.to_broadcast([P, NH])).then_inc(misc_in, 16)
            act.dma_start(rt_w[:, :, :], m_router[0].rearrange("(k p) e -> p k e", p=P)).then_inc(misc_in, 16)

            act.wait_ge(consts, CONSTS)
            act.wait_ge(cols_ready, 1)
            then(nc.scalar.activation(cact[:, :], cols[:, CB_C:CB_C + 8], ACT.Silu), Signal(cact_ready))
            h_sig, sqs, rmss = Signal(h_done), Signal(sq_done), Signal(rms_done)

            def norm(q, affines):
                for i in range(4):
                    act.wait_ge(x_new, 4 * q + i + 1)
                    then(nc.scalar.activation(B[:, 2 * i:2 * i + 2, :], xT[:, 2 * i:2 * i + 2, :], ACT.Square), sqs)
                act.wait_ge(stat_mm, q + 1)
                then(nc.scalar.activation(rms[:, :], bank[4][:, 0:SEQ], ACT.Sqrt, bias=eps[:, 0:1]), rmss)
                act.wait_ge(mod_ready, q + 1)
                for dst, a0, sh0 in affines:
                    for k in range(KC):
                        act.wait_ge(xn_done, 4 * q + k // 2 + 1)
                        then(nc.scalar.activation(dst[:, k, :], A[:, k, :], ACT.Identity, scale=aff[:, a0 + k:a0 + k + 1],
                                                  bias=mod[:, sh0 + k:sh0 + k + 1]), h_sig)

            norm(0, [(H, 0, 0)])
            la = Signal(lam_a)
            then(nc.scalar.activation(lru[:, 0, :], cols[:, CB_LAM:CB_LAM + 8], ACT.Abs), la)
            then(nc.scalar.activation(lru[:, 1, :], lru[:, 0, :], ACT.Exp, scale=-1.0), la)
            act.wait_ge(lam_d, 1)
            then(nc.scalar.activation(lru[:, 3, :], lru[:, 2, :], ACT.Ln), la)

            def gelu(T, i):
                act.wait_ge(acc_full[T % 2], T // 2 + 1)
                ins = nc.scalar.activation(B[:, 2 * i:2 * i + 2, :], bank[T % 2][:, :].rearrange("p (a n) -> p a n", a=2),
                                           ACT.Gelu_apprx_tanh)
                ins.then_inc(acc_free[T % 2], 1)
                act.wait_ge(acc_free[T % 2], T // 2 + 1)

            gelu(4, 0)
            gelu(5, 1)
            for k in range(KC):
                T = 6 + k
                act.wait_ge(acc_full[T % 2], T // 2 + 1)
                then(nc.scalar.activation(A[:, k, :], bank[T % 2][:, 0:SEQ], ACT.Sigmoid,
                                          bias=cols[:, CB_GAB + k:CB_GAB + k + 1]))
                ins = nc.scalar.activation(G[:, k, :], bank[T % 2][:, SEQ:2 * SEQ], ACT.Sigmoid,
                                           bias=cols[:, CB_GXB + k:CB_GXB + k + 1])
                ins.then_inc(acc_free[T % 2], 1)
                act.wait_ge(acc_free[T % 2], T // 2 + 1)
            act.wait_ge(lam_d, 2)
            ls = Signal(lru_a)
            for k in range(KC):
                then(nc.scalar.activation(Dd[:, k, :], A[:, k, :], ACT.Tanh, scale=s8[:, k:k + 1]))
            for k in range(KC):
                then(nc.scalar.activation(A[:, k, :], A[:, k, :], ACT.Exp, scale=s8[:, k:k + 1]), ls)
            gelu(14, 2)
            gelu(15, 3)
            bt = Signal(lru_beta)
            for k in range(KC):
                act.wait_ge(lru_var, k + 1)
                then(nc.scalar.activation(Dd[:, k, :], Dd[:, k, :], ACT.Sqrt, scale=-1.0), bt)

            norm(1, [])
            for k in range(KC):
                act.wait_ge(fx_ready, k + 1)
                nc.scalar.activation(fh[:, k, :], A[:, k, :], ACT.Copy).then_inc(fh_ready, 1)
            for n, (t, part) in enumerate(dense_steps):
                if part == 0 or (part == 4 and t % 2 == 0):
                    slot, at = full_at[name_of[("gu", t) if part == 0 else ("down", t // 2)]]
                    act.wait_ge(ring_full[slot], at)
                if n >= WB:
                    act.wait_ge(dense_used, n - WB + 1)
                nc.scalar.activation(dhi[:, n % WB, :], dense_raw(t, part), ACT.Copy).then_inc(dhi_ready, 1)
                m = t - 1 if part < 4 else t
                if (part == 0 and t) or (m == PAIRS_DENSE - 1 and part == 4):
                    act.wait_ge(dense_used, dense_steps.index((m, 3)) + 1)
                    after(act, gl_ready, m)
                    for i in range(2):
                        nc.scalar.activation(silu[:, i, :], bank[i][:, 0:SEQ], ACT.Silu).then_inc(silu_done, 1)
                if (part == 1 and t) or (m == PAIRS_DENSE - 1 and part == 4):
                    act.wait_ge(hid_done, m + 1)
                    nc.scalar.activation(gh[:, m % 2, :, :], silu[:, :, :], ACT.Copy).then_inc(gh_ready, 1)
            ra = Signal(rope_a)
            act.wait_ge(rope_d, 1)
            then(nc.scalar.activation(sin2[:, :, 32:64], ang[:, :, :], ACT.Sin), ra)
            then(nc.scalar.activation(turn[:, :, :], ang[:, :, :], ACT.Abs), ra)
            then(nc.scalar.activation(cos2[:, :, 0:32], turn[:, :, :], ACT.Sin, scale=-1.0, bias=half_pi[:, 0:1]), ra)

            norm(2, [(H, 16, 48), (C, 24, 64)])
            qs, rq, qk = Signal(qsq_done), Signal(rq_done), Signal(qkT_done)

            def squares(T):
                w = 256 if T < 2 else UC
                a = 20 + T
                act.wait_ge(acc_full[a % 2], a // 2 + 1)
                if T == 1:
                    act.wait_ge(ada_mm, 26)
                if T >= 2:
                    act.wait_ge(ss_done, T - 1)
                then(nc.scalar.activation(sqb[:, T % 2, 0:w], bank[a % 2][:, 0:w], ACT.Square), qs)

            def roots(T):
                nh = 4 if T < 2 else 8
                act.wait_ge(ss_done, T + 1)
                then(nc.scalar.activation(ssq[:, T % 2, 0:nh], ssq[:, T % 2, 0:nh], ACT.Sqrt, scale=1.0 / HD,
                                          bias=eps[:, 0:1]), rq)

            def copy_T(T):
                act.wait_ge(qk_tp, T + 1)
                dst = kT if T < 2 else B
                c0, n = (0, T) if T < 2 else (4 * ((T - 2) // 2), T % 2)
                then(nc.scalar.activation(dst[:, c0:c0 + 4, n * P:(n + 1) * P],
                                          bank[5 + T % 2][:, :].rearrange("p (a n) -> p a n", a=4), ACT.Copy), qk)

            for T in range(6):
                squares(T)
                roots(T)
                if T:
                    copy_T(T - 1)
            copy_T(5)

            ex, pt, oe = Signal(exp_done), Signal(pT_evac), Signal(o_evac)

            def exps(h):
                act.wait_ge(nm_done, h + 1)
                then(nc.scalar.activation(Pb[:, h % 4, 0:P], Pb[:, h % 4, 0:P], ACT.Exp, bias=nm[:, h, 0:1],
                                          accum_out=sm[:, h, 0:1]))
                then(nc.scalar.activation(Pb[:, h % 4, P:3 * P], Pb[:, h % 4, P:3 * P], ACT.Exp, bias=nm[:, h, 1:2],
                                          accum_out=sm[:, h, 1:2]))
                then(nc.scalar.activation(es[:, h, :], nm[:, h, :], ACT.Exp, bias=sinks[:, h:h + 1]), ex)

            def copy_p(h):
                act.wait_ge(pT_mm, h + 1)
                if h >= 2:
                    act.wait_ge(pv_mm, h - 1)
                then(nc.scalar.activation(PT[:, h % 2, 0:3 * P], bank[7 if h % 2 else 4][:, 0:3 * P], ACT.Copy), pt)

            def copy_o(k):
                act.wait_ge(pv_mm, 2 * k + 2)
                then(nc.scalar.activation(A[:, k, :], bank[k % 2][:, 0:SEQ], ACT.Copy), oe)

            exps(0)
            exps(1)
            for h in range(NH):
                if h + 2 < NH:
                    exps(h + 2)
                copy_p(h)
                if h >= 2 and h % 2 == 0:
                    copy_o(h // 2 - 1)
            copy_o(NH // 2 - 1)

            norm(3, [(H, 32, 88)])
            ht = Signal(ht_done)
            for i in range(4):
                act.wait_ge(ht_tp, i + 1)
                then(nc.scalar.activation(htok[:, i // 2, 512 * (i % 2):512 * (i % 2) + 512], bank[6 + i % 2][:, :],
                                          ACT.Copy), ht)
            act.wait_ge(rt_d, 1)
            then(nc.scalar.activation(rts[:, 4, :], rts[:, 3, :], ACT.Exp), Signal(rt_a))

            def take(g):
                act.wait_ge(xg_mm, g + 1)
                for i in range(2):
                    nc.scalar.activation(xh[:, 4 * i:4 * i + 4, :],
                                         bank[6 + i][:, :].rearrange("p (k s) -> p k s", k=4),
                                         ACT.Copy).then_inc(xh_ready, 1)

            def job(j, e, blk=0, extra=False):
                if extra:
                    take(j + 1)
                for n, (t, part) in enumerate(step_order()):
                    if part == 0 or (part == 4 and t % 2 == 0):
                        i = unit_of(t, part)
                        act.wait_ge(ring_full[i % RING], j * per_job[i % RING] + landed_at[i])
                    if not (isinstance(j, int) and n < WB):
                        act.wait_ge(step_used, j * STEPS + (n - WB + 1))
                    nc.scalar.activation(whi[:, n % WB, :], raw(t, part), ACT.Copy).then_inc(hi_ready, 1)
                    if n == 2 and not extra and not (isinstance(j, int) and j == 0):
                        y_out(j - 1)
                    if (part == 1 and t) or (t == PAIRS - 1 and part == 4):
                        m = t - 1 if part == 1 else t
                        act.wait_ge(step_used, j * STEPS + (6 * m + 2 if m else 4))
                        nc.scalar.activation(silu[:, m % 2, :], bank[m % 2][:, 0:2 * P], ACT.Silu).then_inc(silu_ready, 1)
                    if part == 4 and t < PAIRS - 1:
                        hidden_hi(j, t)
                    if t == 0 and part == 5:
                        act.wait_ge(selT_mm, j + 1)
                        nc.scalar.activation(selT[:, :], bank[3][:, 0:SEQ], ACT.Copy).then_inc(selT_ready, 1)
                if not extra:
                    take(j + 1)
                hidden_hi(j, PAIRS - 1)
                if extra:
                    y_out(j)

            def y_out(j):
                act.wait_ge(step_used, j * STEPS + STEPS)
                nc.scalar.activation(y[:, 0:512], bank[4][:, :], ACT.Copy).then_inc(y_a, 1)

            def hidden_hi(j, t):
                act.wait_ge(hT_mm, j * PAIRS + (t + 1))
                nc.scalar.activation(hh[:, t % 2, :, :], bank[2 + t % 2][:, 0:2 * CAP].rearrange("p (i s) -> p i s", i=2),
                                     ACT.Copy).then_inc(hh_ready, 1)

            take(0)
            job(0, 0)
            with act.Fori(1, E) as e:
                job(e, e)
            y_out(E - 1)
            act.wait_ge(cnt_ready, 1)
            more_jobs(act, job, extra=True)
            fe = Signal(fin_evac)
            for i in range(4):
                act.wait_ge(fin_tp, i + 1)
                then(nc.scalar.activation(otok[:, i // 2, 512 * (i % 2):512 * (i % 2) + 512], bank[6 + i % 2][:, :],
                                          ACT.Copy), fe)

        @block.vector
        def _(dve):
            step = Signal(dve_step)
            v_ = nc.vector

            def then(ins, signal=None):
                s = signal or step
                s.up(ins)
                dve.wait_ge(s.sem, s.n)

            dve.wait_ge(par_tp, 1)
            then(v_.tensor_copy(cols[:, 0:P + NB_ROWS], bank[5][:, 0:P + NB_ROWS]), Signal(cols_ready))
            xs = Signal(x_new)
            for i in range(4):
                dve.wait_ge(x_tp, i + 1)
                then(v_.tensor_copy(xT[:, 2 * i:2 * i + 2, :],
                                    bank[(0, 1, 6, 7)[i]][:, :].rearrange("p (a n) -> p a n", a=2)), xs)
            ad, mr = Signal(ada_done), Signal(mod_ready)

            def affine(a0, sc0, g0, signal=None):
                then(v_.scalar_tensor_tensor(out=aff[:, a0:a0 + 8], in0=mod[:, sc0:sc0 + 8], scalar=1.0,
                                             in1=cols[:, g0:g0 + 8], op0=ALU.add, op1=ALU.mult), signal)

            def gate(i, g0):
                then(v_.tensor_scalar(gate1[:, 8 * i:8 * i + 8], mod[:, g0:g0 + 8], 1.0, None, ALU.add))

            asum = Signal(ada_sum)

            def ada_chunks(v):
                for k in range(KC):
                    ada_chunk(v, k)

            def ada_chunk(v, k):
                slot, at = full_at[name_of[("ada", v)]]
                w = ring[slot][:, 0:KC * UC].rearrange("p (k n) -> p k n", k=KC)[:, k, :]
                if k == 0:
                    if v >= 4:
                        dve.wait_ge(ada_mm, v - 3)
                    dve.wait_ge(ring_full[slot], at)
                    then(v_.tensor_scalar(ada_acc(v), w, cact[:, 0:1], None, ALU.mult))
                else:
                    then(v_.scalar_tensor_tensor(out=ada_acc(v), in0=w, scalar=cact[:, k:k + 1], in1=ada_acc(v),
                                                 op0=ALU.mult, op1=ALU.add), asum if k == KC - 1 else None)

            def ada(v):
                dve.wait_ge(ada_mm, v + 1)
                then(v_.tensor_tensor(mod[:, 4 * v:4 * v + 4], bank[2 + v % 2][:, 0:4], cols[:, 4 * v:4 * v + 4],
                                      ALU.add), ad)
                if v == 3:
                    affine(0, 8, CA_MIX, mr)
                elif v == 5:
                    gate(0, 16)
                elif v == 9:
                    affine(8, 32, CB_FFN, mr)
                elif v == 11:
                    gate(1, 40)
                elif v == 15:
                    affine(16, 56, CB_KVN)
                elif v == 19:
                    affine(24, 72, CA_MIX + 8, mr)
                elif v == 21:
                    gate(2, 80)
                elif v == 25:
                    affine(32, 96, CB_FFN + 8, mr)
                elif v == 27:
                    gate(3, 104)

            xn = Signal(xn_done)

            def norm(q):
                dve.wait_ge(rms_done, q + 1)
                then(v_.reciprocal(rstd[:, :], rms[:, :]))
                for i in range(4):
                    then(v_.tensor_tensor(A[:, 2 * i:2 * i + 2, :], xT[:, 2 * i:2 * i + 2, :],
                                          rstd[:, None, :].to_broadcast([P, 2, SEQ]), ALU.mult), xn)

            dve.wait_ge(cact_ready, 1)
            ada_chunks(0)
            norm(0)
            ada_chunks(2)
            ada(0)
            ada_chunks(3)
            for v in range(1, 4):
                ada(v)
            ld = Signal(lam_d)
            dve.wait_ge(lam_a, 2)
            then(v_.tensor_scalar(lru[:, 2, :], lru[:, 1, :], 1.0, None, ALU.add), ld)
            then(v_.tensor_scalar(lru[:, 4, :], lru[:, 2, :], -1.0, None, ALU.add))
            then(v_.tensor_scalar(lru[:, 5, :], lru[:, 4, :], 0.0, None, ALU.is_equal))
            then(v_.tensor_tensor(lru[:, 4, :], lru[:, 4, :], lru[:, 5, :], ALU.add))
            then(v_.reciprocal(lru[:, 4, :], lru[:, 4, :]))
            dve.wait_ge(lam_a, 3)
            then(v_.tensor_tensor(lru[:, 4, :], lru[:, 4, :], lru[:, 3, :], ALU.mult))
            then(v_.tensor_tensor(lru[:, 4, :], lru[:, 4, :], lru[:, 5, :], ALU.add))
            then(v_.tensor_tensor(lru[:, 4, :], lru[:, 4, :], lru[:, 1, :], ALU.mult))
            then(v_.tensor_scalar(lru[:, 6, :], cols[:, CB_LAM:CB_LAM + 8], -1.0, 0.0, ALU.mult, ALU.max))
            then(v_.tensor_tensor(lru[:, 4, :], lru[:, 4, :], lru[:, 6, :], ALU.add))
            then(v_.tensor_scalar(s8, lru[:, 4, :], -LRU_C, None, ALU.mult), ld)
            dve.wait_ge(misc_in, 96)
            then(v_.tensor_copy(posf[:, :], pos_i[:, :]))
            for n in range(NB):
                then(v_.tensor_scalar(ang[:, n, :], inv_bc[:, :], posf[:, n:n + 1], None, ALU.mult))
            then(v_.tensor_scalar(turn[:, :, :], ang[:, :, :], 1.0 / (2 * math.pi), None, ALU.mult))
            then(v_.tensor_copy(turn_i[:, :, :], turn[:, :, :]))
            then(v_.tensor_copy(turn[:, :, :], turn_i[:, :, :]))
            for part in TWO_PI:
                then(v_.scalar_tensor_tensor(out=ang[:, :, :], in0=turn[:, :, :], scalar=-part, in1=ang[:, :, :],
                                             op0=ALU.mult, op1=ALU.add))
            for edge, op in ((3.1415925, ALU.min), (-3.1415925, ALU.max)):
                last = v_.tensor_scalar(ang[:, :, :], ang[:, :, :], edge, None, op)
                if op == ALU.min:
                    then(last)
            then(last, Signal(rope_d))

            cv = Signal(conv_done)
            for k in range(KC):
                T, half = k // 2, bank[(k // 2) % 2][:, SEQ * (k % 2):SEQ * (k % 2) + SEQ]
                if k % 2 == 0:
                    dve.wait_ge(acc_full[T % 2], T // 2 + 1)
                w = [cols[:, CB_CONVW + 8 * t + k:CB_CONVW + 8 * t + k + 1] for t in range(4)]
                then(v_.tensor_scalar(C[:, k, :], half, w[3], cols[:, CB_CONVB + k:CB_CONVB + k + 1], ALU.mult, ALU.add))
                for lag in (1, 2, 3):
                    ins = v_.scalar_tensor_tensor(out=C[:, k, lag:], in0=half[:, 0:SEQ - lag], scalar=w[3 - lag],
                                                  in1=C[:, k, lag:], op0=ALU.mult, op1=ALU.add)
                    if lag < 3:
                        then(ins)
                    elif k % 2 == 0:
                        then(ins, cv)
                    else:
                        ins.then_inc(acc_free[T % 2], 1)
                        dve.wait_ge(acc_free[T % 2], T // 2 + 1)
                        if T < 2:
                            ada_chunks(4 + T)
            var, mxd = Signal(lru_var), Signal(mix_done)
            for k in range(KC):
                dve.wait_ge(lru_a, k + 1)
                then(v_.tensor_tensor(lt[:, k % 2, :], A[:, k, :], A[:, k, :], ALU.mult))
                then(v_.scalar_tensor_tensor(out=Dd[:, k, :], in0=lt[:, k % 2, :], scalar=1.0, in1=Dd[:, k, :],
                                             op0=ALU.add, op1=ALU.mult), var)
            for k in range(KC):
                then(v_.tensor_tensor(G[:, k, :], G[:, k, :], C[:, k, :], ALU.mult))
                dve.wait_ge(lru_beta, k + 1)
                then(v_.tensor_tensor(G[:, k, :], G[:, k, :], Dd[:, k, :], ALU.mult))
                then(v_.tensor_tensor_scan(C[:, k, :], A[:, k, :], G[:, k, :], 0.0, ALU.mult, ALU.add))
                then(v_.tensor_tensor(C[:, k, :], C[:, k, :], B[:, k, :], ALU.mult), mxd)

            def residual(T0, g, between=lambda i: None):
                for T in range(T0, T0 + 4):
                    between(T - T0)
                    dve.wait_ge(acc_full[T % 2], T // 2 + 1)
                    for a in range(2):
                        k = 2 * (T - T0) + a
                        ins = v_.scalar_tensor_tensor(out=xT[:, k, :], in0=bank[T % 2][:, SEQ * a:SEQ * a + SEQ],
                                                      scalar=gate1[:, 8 * g + k:8 * g + k + 1], in1=xT[:, k, :],
                                                      op0=ALU.mult, op1=ALU.add)
                        if a == 0:
                            then(ins)
                        else:
                            then(ins, xs)

            for v in range(4, 6):
                ada(v)
            residual(16, 0, lambda i: ada_chunks(6 + i))
            for v in range(6, 10):
                ada(v)
            norm(1)
            for k in range(KC):
                v_.tensor_scalar(A[:, k, :], A[:, k, :], aff[:, 8 + k:9 + k], mod[:, 24 + k:25 + k],
                                 ALU.mult, ALU.add).then_inc(fx_ready, 1)
            for k in range(KC):
                dve.wait_ge(fh_ready, k + 1)
                v_.tensor_tensor(fl[:, k, :], A[:, k, :], fh[:, k, :].bitcast(F32), ALU.subtract).then_inc(fl_ready, 1)
            for n, (t, part) in enumerate(dense_steps):
                dve.wait_ge(dhi_ready, n + 1)
                v_.tensor_tensor(dlo[:, n % WB, :], dense_raw(t, part), dhi[:, n % WB, :].bitcast(F32),
                                 ALU.subtract).then_inc(dlo_ready, 1)
                m = t - 1 if part < 4 else t
                if (part == 0 and t) or (m == PAIRS_DENSE - 1 and part == 4):
                    for i in range(2):
                        dve.wait_ge(silu_done, 2 * m + i + 1)
                        ins = v_.tensor_tensor(silu[:, i, :], silu[:, i, :], bank[i][:, SEQ:2 * SEQ], ALU.mult)
                    ins.then_inc(hid_done, 1)
                if (part == 1 and t) or (m == PAIRS_DENSE - 1 and part == 4):
                    dve.wait_ge(gh_ready, m + 1)
                    v_.tensor_tensor(gl[:, m % 2, :, :], silu[:, :, :], gh[:, m % 2, :, :].bitcast(F32),
                                     ALU.subtract).then_inc(gl_ready, 1)
                if part == 3 and t:
                    for v in ada_summed_by(t - 1):
                        ada(v)
                for v, k in ada_ops_beside(n):
                    ada_chunk(v, k)
            for t in (PAIRS_DENSE - 1, PAIRS_DENSE):
                for v in ada_summed_by(t):
                    ada(v)
            dve.wait_ge(dense_used, DSTEPS)
            for i in range(4):
                for a in range(2):
                    k = 2 * i + a
                    then(v_.scalar_tensor_tensor(out=xT[:, k, :], in0=bank[4 + i][:, SEQ * a:SEQ * a + SEQ],
                                                 scalar=gate1[:, 8 + k:9 + k], in1=xT[:, k, :],
                                                 op0=ALU.mult, op1=ALU.add), xs if a else None)
            dve.wait_ge(rope_a, 3)
            then(v_.tensor_copy(cos2[:, :, 32:64], cos2[:, :, 0:32]))
            then(v_.tensor_scalar(sin2[:, :, 0:32], sin2[:, :, 32:64], -1.0, None, ALU.mult))
            norm(2)

            ss, rp = Signal(ss_done), Signal(rope_done)

            def qk(T):
                k_task, n, a = T < 2, T % 2, 20 + T
                nh = 4 if k_task else 8
                w = nh * HD
                ps = bank[a % 2][:, 0:w].rearrange("p (h d) -> p h d", d=HD)
                q_ = qw[:, T % 2, 0:w].rearrange("p (h d) -> p h d", d=HD)
                dve.wait_ge(qsq_done, T + 1)
                if k_task:
                    then(v_.tensor_copy(vt[:, n, :], bank[a % 2][:, 256:512]))
                if T >= 2:
                    dve.wait_ge(qk_tp, T - 1)
                gain = (kg if k_task else qg)[:, None, :].to_broadcast([P, nh, HD])
                ins = v_.tensor_tensor(q_, ps, gain, ALU.mult)
                ins.then_inc(acc_free[a % 2], 1)
                dve.wait_ge(acc_free[a % 2], ACC_FREE_AT[a])
                then(v_.tensor_reduce(ssq[:, T % 2, 0:nh], sqb[:, T % 2, 0:w].rearrange("p (h d) -> p h d", d=HD),
                                      AX.X, ALU.add), ss)
                dve.wait_ge(rq_done, T + 1)
                then(v_.reciprocal(ssq[:, T % 2, 0:nh], ssq[:, T % 2, 0:nh]))
                then(v_.tensor_tensor(q_, q_, ssq[:, T % 2, 0:nh][:, :, None].to_broadcast([P, nh, HD]), ALU.mult))
                r_ = rtmp[:, 0:w].rearrange("p (h d) -> p h d", d=HD)
                sn = sin2[:, n, None, :].to_broadcast([P, nh, HD])
                then(v_.tensor_tensor(r_[:, :, 0:32], q_[:, :, 32:64], sn[:, :, 0:32], ALU.mult))
                then(v_.tensor_tensor(r_[:, :, 32:64], q_[:, :, 0:32], sn[:, :, 32:64], ALU.mult))
                then(v_.tensor_tensor(q_, q_, cos2[:, n, None, :].to_broadcast([P, nh, HD]), ALU.mult))
                if k_task:
                    then(v_.tensor_tensor(kdup[:, n, :, 0, :], q_, r_, ALU.add))
                    then(v_.tensor_tensor(kdup[:, n, :, 1, :], q_, r_, ALU.add), rp)
                else:
                    then(v_.tensor_tensor(q_, q_, r_, ALU.add), rp)

            ada_chunks(25)
            for T in range(6):
                qk(T)
                if T == 1:
                    ada(25)

            sce, nms, pns = Signal(sc_evac), Signal(nm_done), Signal(pn_done)

            def scores(h):
                dve.wait_ge(sc_mm, h + 1)
                if h >= 4:
                    dve.wait_ge(pT_mm, h - 3)
                p_ = Pb[:, h % 4, :]
                then(v_.scalar_tensor_tensor(out=p_, in0=bank[5 + h % 2][:, 0:3 * P], scalar=HD ** -0.5,
                                             in1=mask[:, :], op0=ALU.mult, op1=ALU.add), sce)
                then(v_.tensor_reduce(mx[:, h, 0:1], p_[:, 0:P], AX.X, ALU.max))
                then(v_.tensor_reduce(mx[:, h, 1:2], p_[:, P:3 * P], AX.X, ALU.max))
                then(v_.tensor_scalar(nm[:, h, :], mx[:, h, :], sinks[:, h:h + 1], -1.0, ALU.max, ALU.mult), nms)

            def probs(h):
                dve.wait_ge(exp_done, h + 1)
                then(v_.tensor_tensor(sm[:, h, :], sm[:, h, :], es[:, h, :], ALU.add))
                then(v_.reciprocal(sm[:, h, :], sm[:, h, :]))
                then(v_.tensor_scalar(Pb[:, h % 4, 0:P], Pb[:, h % 4, 0:P], sm[:, h, 0:1], None, ALU.mult))
                then(v_.tensor_scalar(Pb[:, h % 4, P:3 * P], Pb[:, h % 4, P:3 * P], sm[:, h, 1:2], None, ALU.mult), pns)

            scores(0)
            scores(1)
            for h in range(NH):
                if h + 2 < NH:
                    scores(h + 2)
                probs(h)
            dve.wait_ge(qk_tp, 6)
            residual(26, 2, lambda i: ada_chunks(26 + i) if i < 2 else None)
            norm(3)
            for v in (26, 27):
                ada(v)

            R = lambda i: rt[:, i, :, 0:E]
            then(v_.memset(rt[:, 9:12, :, E:E + 1], 0.0))
            col = lambda i: rts[:, i, :]
            idx = iota[:, None, 0:E].to_broadcast([P, NB, E])
            bc = lambda i: rts[:, i, :][:, :, None].to_broadcast([P, NB, E])
            dve.wait_ge(rt_mm, 1)
            then(v_.tensor_copy(R(0), bank[5][:, 0:NB * E].rearrange("p (b e) -> p b e", b=NB)))
            for r in range(2):
                lg, oh = R(3 * r), R(3 * r + 2)
                then(v_.tensor_reduce(col(r), lg, AX.X, ALU.max))
                then(v_.tensor_tensor(R(1), lg, bc(r), ALU.is_equal))
                then(v_.scalar_tensor_tensor(out=R(1), in0=R(1), scalar=-64.0, in1=idx, op0=ALU.mult, op1=ALU.add))
                then(v_.tensor_reduce(col(2), R(1), AX.X, ALU.min))
                then(v_.tensor_tensor(oh, R(1), bc(2), ALU.is_equal))
                if r == 0:
                    then(v_.scalar_tensor_tensor(out=R(3), in0=oh, scalar=-3e38, in1=lg, op0=ALU.mult, op1=ALU.add))
            then(v_.tensor_tensor(msk, R(2), R(5), ALU.add), Signal(mask_ready))
            then(v_.tensor_tensor(col(3), col(1), col(0), ALU.subtract), Signal(rt_d))
            dve.wait_ge(rt_a, 1)
            then(v_.tensor_scalar(col(5), col(4), 1.0, None, ALU.add))
            then(v_.reciprocal(col(5), col(5)))
            then(v_.tensor_tensor(col(6), col(5), col(4), ALU.mult))
            then(v_.tensor_tensor(R(6), R(2), bc(5), ALU.mult))
            then(v_.tensor_tensor(R(7), R(5), bc(6), ALU.mult))
            then(v_.tensor_tensor(gates, R(6), R(7), ALU.add))
            dve.wait_ge(pos_mm, 1)
            then(v_.tensor_copy(pos, bank[4][:, 0:NB * E].rearrange("p (b e) -> p b e", b=NB)))
            then(v_.tensor_reduce(rts[:, 7, 0:1], bank[4][:, NB * E:NB * E + E], AX.X, ALU.max))
            then(v_.tensor_copy(cnt_i[:, E:E + 1], rts[:, 7, 0:1]))
            then(v_.tensor_copy(cnt_i[:, 0:E], bank[4][:, NB * E:NB * E + E]), Signal(cnt_ready))

            def select(g, e, blk):
                after(dve, xg_mm, g)
                for n in range(NB):
                    ins = v_.tensor_scalar(sel[:, n, :], iota[:, blk * CAP:(blk + 1) * CAP],
                                           rt[:, 10, n, bass.ds(e, 1)], rt[:, 11, n, bass.ds(e, 1)],
                                           ALU.is_equal, ALU.mult)
                ins.then_inc(sel_ready, 1)

            def rest(g):
                for i in range(2):
                    dve.wait_ge(xh_ready, g * 2 + (i + 1))
                    v_.tensor_tensor(xl[:, 4 * i:4 * i + 4, :], bank[6 + i][:, :].rearrange("p (k s) -> p k s", k=4),
                                     xh[:, 4 * i:4 * i + 4, :].bitcast(F32), ALU.subtract).then_inc(xl_ready, 1)

            def hidden_lo(j, t):
                dve.wait_ge(hh_ready, j * PAIRS + (t + 1))
                v_.tensor_tensor(hl[:, t % 2, :, :], bank[2 + t % 2][:, 0:2 * CAP].rearrange("p (i s) -> p i s", i=2),
                                 hh[:, t % 2, :, :].bitcast(F32), ALU.subtract).then_inc(hl_ready, 1)

            def job(j, e, blk=0, extra=False):
                if extra:
                    select(j + 1, e, blk)
                    rest(j + 1)
                for n, (t, part) in enumerate(step_order()):
                    dve.wait_ge(hi_ready, j * STEPS + (n + 1))
                    v_.tensor_tensor(wlo[:, n % WB, :], raw(t, part), whi[:, n % WB, :].bitcast(F32),
                                     ALU.subtract).then_inc(lo_ready, 1)
                    if not extra and not (isinstance(j, int) and j == 0):
                        if n == 2:
                            y_out(j - 1)
                        elif n == 5:
                            add_output(j - 1)
                    if (part == 1 and t) or (t == PAIRS - 1 and part == 4):
                        m = t - 1 if part == 1 else t
                        dve.wait_ge(silu_ready, j * PAIRS + (m + 1))
                        v_.tensor_tensor(hs[:, m % 2, :], silu[:, m % 2, :], bank[m % 2][:, 2 * P:4 * P],
                                         ALU.mult).then_inc(hs_ready, 1)
                    if part == 4 and t < PAIRS - 1:
                        hidden_lo(j, t)
                    if t == 1 and part == 0:
                        after(dve, selT_mm, j)
                        for b in range(NB):
                            ins = v_.tensor_scalar(selg[:, b, :], iota[:, blk * CAP:(blk + 1) * CAP],
                                                   rt[:, 10, b, bass.ds(e, 1)], rt[:, 9, b, bass.ds(e, 1)],
                                                   ALU.is_equal, ALU.mult)
                        ins.then_inc(selg_ready, 1)
                    if t == PAIRS - 3 and part == 5 and not extra:
                        select(j + 1, e + 1, 0)
                if not extra:
                    rest(j + 1)
                hidden_lo(j, PAIRS - 1)
                if extra:
                    y_out(j)
                    add_output(j)

            def y_out(j):
                dve.wait_ge(step_used, j * STEPS + STEPS)
                v_.tensor_copy(y[:, 512:1024], bank[5][:, :]).then_inc(y_d, 1)

            def add_output(j):
                after(dve, back_done, j * 8)
                for i in range(4):
                    dve.wait_ge(back_mm, j * 4 + (i + 1))
                    for a in range(2):
                        k = 2 * i + a
                        v_.scalar_tensor_tensor(out=xT[:, k, :], in0=bank[2 + i % 2][:, SEQ * a:SEQ * a + SEQ],
                                                scalar=gate1[:, 24 + k:25 + k], in1=xT[:, k, :],
                                                op0=ALU.mult, op1=ALU.add).then_inc(back_done, 1)

            select(0, 0, 0)
            rest(0)
            job(0, 0)
            with dve.Fori(1, E) as e:
                job(e, e)
            y_out(E - 1)
            add_output(E - 1)
            more_jobs(dve, job, extra=True)
            then(v_.tensor_copy(rts[:, 7, :], rts[:, 6, :]), Signal(x_final))

        @block.tensor
        def _(pe):
            mm = nc.tensor.matmul

            def transposed(dst, src, i=ident):
                return nc.tensor.transpose(dst, src, i)

            pe.wait_ge(consts, CONSTS)
            pe.wait_ge(par_in, 16 * len(rows))
            transposed(bank[5][:, 0:P], pa_rows[:, :], ident[:, :])
            transposed(bank[5][:, P:P + NB_ROWS], pb_rows[0:NB_ROWS, :], ident[0:NB_ROWS, 0:NB_ROWS]).then_inc(par_tp, 1)
            pe.wait_ge(x_in, 16)
            for i in range(4):
                for a in range(2):
                    for n in range(NB):
                        last = transposed(bank[(0, 1, 6, 7)[i]][:, (2 * a + n) * P:(2 * a + n + 1) * P],
                                          xin[:, n, (2 * i + a) * P:(2 * i + a + 1) * P], ident[:, :])
                last.then_inc(x_tp, 1)

            def arrived(name):
                s, at = full_at[name_of[name]]
                pe.wait_ge(ring_full[s], at)
                return ring[s]

            def columns(name):
                return arrived(name)[:, 0:KC * UC].rearrange("p (k n) -> p k n", k=KC)

            tasks = [0]

            def acc_bank():
                T = tasks[0]
                tasks[0] += 1
                if T >= 2:
                    wait_free(pe, T - 2)
                return T, bank[T % 2]

            def stats(q):
                for k in range(KC):
                    if k % 2 == 0:
                        pe.wait_ge(sq_done, 4 * q + k // 2 + 1)
                    last = mm(bank[4][:, 0:SEQ], mean_w[:, :], B[:, k, :], start=k == 0, stop=k == KC - 1)
                last.then_inc(stat_mm, 1)

            def ada(v):
                if v >= 2:
                    pe.wait_ge(ada_done, v - 1)
                if v == ADA_ON_PE:
                    w = columns(("ada", v))
                    for i in range(UC // P):
                        for k in range(KC):
                            last = mm(bank[2 + v % 2][:, i:i + 1], w[:, k, i * P:(i + 1) * P], cact[:, k:k + 1],
                                      start=k == 0, stop=k == KC - 1)
                    last.then_inc(ada_mm, 1)
                    return
                pe.wait_ge(ada_sum, ada_sum_at(v))
                for i in range(UC // P):
                    last = mm(bank[2 + v % 2][:, i:i + 1], ada_acc(v)[:, i * P:(i + 1) * P], ones[:, 0:1],
                              start=True, stop=True)
                last.then_inc(ada_mm, 1)

            def project(name, src, ready=None, r0=0):
                w = columns(name)
                for tk in range(2):
                    T, b = acc_bank()
                    for a in range(2):
                        i = 2 * tk + a
                        for k in range(KC):
                            if ready is not None and tk == 0 and a == 0:
                                pe.wait_ge(ready, r0 + k + 1)
                            last = mm(b[:, SEQ * a:SEQ * a + SEQ], w[:, k, i * P:(i + 1) * P], src[:, k, :],
                                      start=k == 0, stop=k == KC - 1)
                    last.then_inc(acc_full[T % 2], 1)

            stats(0)
            for v in range(4):
                ada(v)
            for i in range(3):
                project(("in", i), H, h_done if i == 0 else None)
            w = arrived("gates")
            for k in range(KC):
                T, b = acc_bank()
                if k % 2 == 0:
                    pe.wait_ge(conv_done, k // 2 + 1)
                else:
                    wait_free(pe, k // 2)
                mm(b[:, 0:SEQ], w[:, k * P:(k + 1) * P], C[:, k, :], start=True, stop=True)
                mm(b[:, SEQ:2 * SEQ], w[:, 1024 + k * P:1024 + (k + 1) * P], C[:, k, :], start=True,
                   stop=True).then_inc(acc_full[T % 2], 1)
            project(("in", 3), H)
            for v in range(4, 6):
                ada(v)
            for i in range(2):
                project(("out", i), C, mix_done if i == 0 else None)
                for v in (6 + 2 * i, 7 + 2 * i):
                    ada(v)
            stats(1)

            def stationary_split(o, w, xs, start, stop):
                hi, lo = dhi[:, w[0], w[1]:w[1] + P], dlo[:, w[0], w[1]:w[1] + P]
                mm(o, hi, xs[0], start=start, stop=False, skip_group_check=True)
                mm(o, hi, xs[1], start=False, stop=False, skip_group_check=True)
                return mm(o, lo, xs[0], start=False, stop=stop, skip_group_check=True)

            for n, (t, part) in enumerate(dense_steps):
                if part == 0 and t:
                    pe.wait_ge(hid_done, t)
                if part == 4:
                    pe.wait_ge(gl_ready, t + 1)
                pe.wait_ge(dlo_ready, n + 1)
                if part < 4:
                    for a in range(2):
                        k = 2 * part + a
                        if t == 0:
                            pe.wait_ge(fl_ready, k + 1)
                        for c in range(4):
                            half, i = c // 2, c % 2
                            last = stationary_split(bank[i][:, SEQ * half:SEQ * (half + 1)], (n % WB, 512 * a + P * c),
                                                    (fh[:, k, :], fl[:, k, :]), k == 0 and half == 0, k == KC - 1)
                else:
                    i = part - 4
                    for k in range(KC):
                        last = stationary_split(bank[4 + k // 2][:, SEQ * (k % 2):SEQ * (k % 2) + SEQ], (n % WB, P * k),
                                                (gh[:, t % 2, i, :], gl[:, t % 2, i, :]),
                                                t == 0 and i == 0 and k % 2 == 0, t == PAIRS_DENSE - 1 and i == 1)
                last.then_inc(dense_used, 1)
                if part == 3:
                    for v in ada_summed_by(t):
                        ada(v)
            for v in ada_summed_by(PAIRS_DENSE):
                ada(v)

            stats(2)
            w_kv_ = columns("kv")
            for n in range(NB):
                T, b = acc_bank()
                for k in range(KC):
                    if n == 0:
                        pe.wait_ge(h_done, 8 + k + 1)
                    last = mm(b[:, :], H[:, k, n * P:(n + 1) * P], w_kv_[:, k, :], start=k == 0, stop=k == KC - 1)
                last.then_inc(acc_full[T % 2], 1)

            def to_T(T):
                pe.wait_ge(rope_done, T + 1)
                if T >= 2:
                    pe.wait_ge(qkT_done, T - 1)
                for i in range(4):
                    src = (kdup[:, T, :, :, :].rearrange("p h t d -> p (h t d)") if T < 2 else qw[:, T % 2, :])
                    last = transposed(bank[5 + T % 2][:, i * P:(i + 1) * P], src[:, i * P:(i + 1) * P], ident[:, :])
                last.then_inc(qk_tp, 1)

            ada(25)
            pe.wait_ge(h_done, 24)
            for hf in range(2):
                wq = columns(("q", hf))
                for n in range(NB):
                    T, b = acc_bank()
                    for k in range(KC):
                        last = mm(b[:, :], C[:, k, n * P:(n + 1) * P], wq[:, k, :], start=k == 0, stop=k == KC - 1)
                    last.then_inc(acc_full[T % 2], 1)
                    to_T(2 * hf + n)
            to_T(4)
            to_T(5)

            def scores(h):
                lo, k, g = HD * (h % 2), h // 2, h // (NH // NKV)
                if h >= 2:
                    pe.wait_ge(sc_evac, h - 1)
                else:
                    pe.wait_ge(qkT_done, 6)
                q_ = B[lo:lo + HD, k, :]
                mm(bank[5 + h % 2][:, 0:P], q_[:, 0:P], kT[lo:lo + HD, g, 0:P], start=True, stop=True)
                mm(bank[5 + h % 2][:, P:3 * P], q_[:, P:2 * P], kT[lo:lo + HD, g, :], start=True,
                   stop=True).then_inc(sc_mm, 1)

            def probs_T(h):
                pe.wait_ge(pn_done, h + 1)
                if h >= 2:
                    pe.wait_ge(pT_evac, h - 1)
                b = bank[7 if h % 2 else 4]
                for i in range(3):
                    last = transposed(b[:, i * P:(i + 1) * P], Pb[:, h % 4, i * P:(i + 1) * P], ident[:, :])
                last.then_inc(pT_mm, 1)

            def values(h):
                lo, k, g = HD * (h % 2), h // 2, h // (NH // NKV)
                pe.wait_ge(pT_evac, h + 1)
                if h % 2 == 0 and k >= 2:
                    pe.wait_ge(o_evac, k - 1)
                o = bank[k % 2][lo:lo + HD, :]
                v0, v1 = vt[:, 0, g * HD:(g + 1) * HD], vt[:, 1, g * HD:(g + 1) * HD]
                p_ = PT[:, h % 2, :]
                mm(o[:, 0:P], v0, p_[:, 0:P], start=True, stop=True)
                mm(o[:, P:2 * P], v0, p_[:, P:2 * P], start=True, stop=False)
                mm(o[:, P:2 * P], v1, p_[:, 2 * P:3 * P], start=False, stop=True).then_inc(pv_mm, 1)

            for h in range(3):
                scores(h)
            for h in range(NH):
                if h + 3 < NH:
                    scores(h + 3)
                probs_T(h)
                if h:
                    values(h - 1)
            values(NH - 1)
            pe.wait_ge(o_evac, KC)
            for i in range(2):
                project(("o", i), A)
            assert tasks[0] == acc_tasks
            stats(3)
            for v in (26, 27):
                ada(v)

            for n in range(NB):
                for k in range(KC):
                    if n == 0:
                        pe.wait_ge(h_done, 24 + k + 1)
                    last = mm(bank[5][:, n * E:(n + 1) * E], H[:, k, n * P:(n + 1) * P], rt_w[:, k, :],
                              start=k == 0, stop=k == KC - 1)
            last.then_inc(rt_mm, 1)
            for i in range(4):
                if i >= 2:
                    pe.wait_ge(ht_done, i - 1)
                for a in range(4):
                    last = transposed(bank[6 + i % 2][:, a * P:(a + 1) * P],
                                      H[:, 4 * (i % 2) + a, (i // 2) * P:(i // 2 + 1) * P], ident[:, :])
                last.then_inc(ht_tp, 1)
            pe.wait_ge(mask_ready, 1)
            mm(bank[4][:, 0:E], before[:, :], msk[:, 0, :], start=True, stop=True)
            mm(bank[4][:, E:2 * E], before[:, :], msk[:, 1, :], start=True, stop=False)
            mm(bank[4][:, E:2 * E], ones[:, :], msk[:, 0, :], start=False, stop=True)
            mm(bank[4][:, 2 * E:3 * E], ones[:, :], msk[:, 0, :], start=True, stop=False)
            mm(bank[4][:, 2 * E:3 * E], ones[:, :], msk[:, 1, :], start=False, stop=True).then_inc(pos_mm, 1)
            for T in (acc_tasks - 2, acc_tasks - 1):
                wait_free(pe, T)
            pe.wait_ge(ht_done, 4)
            pe.wait_ge(cnt_ready, 1)

            def gather(g):
                pe.wait_ge(sel_ready, g + 1)
                after(pe, xl_ready, g * 2)
                for k in range(KC):
                    for n in range(NB):
                        last = mm(bank[6 + k // 4][:, (k % 4) * CAP:(k % 4 + 1) * CAP], htok[:, n, k * P:(k + 1) * P],
                                  sel[:, n, :], start=n == 0, stop=n == NB - 1)
                last.then_inc(xg_mm, 1)

            def split_product(o, hi, lo, w, start, stop):
                b, c0 = w
                mm(o, hi, whi[:, b, c0:c0 + 512], start=start, stop=False)
                mm(o, lo, whi[:, b, c0:c0 + 512], start=False, stop=False)
                return mm(o, hi, wlo[:, b, c0:c0 + 512], start=False, stop=stop)

            def hidden_T(j, t):
                pe.wait_ge(hs_ready, j * PAIRS + (t + 1))
                if t == 0:
                    after(pe, back_done, j * 8)
                elif t == 1:
                    pe.wait_ge(selT_ready, j + 1)
                after(pe, hl_ready, j * PAIRS + max(0, t - 1))
                for i in range(2):
                    last = transposed(bank[2 + t % 2][:, i * P:(i + 1) * P], hs[:, t % 2, i * P:(i + 1) * P], ident[:, :])
                last.then_inc(hT_mm, 1)

            def job(j, e, blk=0, extra=False):
                g = j + 1 if extra else j
                if extra:
                    gather(g)
                pe.wait_ge(xl_ready, g * 2 + 2)
                for n, (t, part) in enumerate(step_order()):
                    if part == 0:
                        after(pe, hs_ready, j * PAIRS + max(0, t - 1))
                    if part == 4:
                        pe.wait_ge(hl_ready, j * PAIRS + (t + 1))
                    pe.wait_ge(lo_ready, j * STEPS + (n + 1))
                    for a in range(2):
                        w = (n % WB, 512 * a)
                        if part < 4:
                            k = 2 * part + a
                            last = split_product(bank[t % 2][:, :], xh[:, k, :], xl[:, k, :], w, k == 0, k == KC - 1)
                        else:
                            i = part - 4
                            last = split_product(bank[4 + a][:, :], hh[:, t % 2, i, :], hl[:, t % 2, i, :], w,
                                                 t == 0 and i == 0, t == PAIRS - 1 and i == 1)
                    last.then_inc(step_used, 1)
                    if t == 0 and part == 3 and not extra and not (isinstance(j, int) and j == 0):
                        back(j - 1)
                    if part == 1 and t:
                        hidden_T(j, t - 1)
                    if t == PAIRS - 2 and part == 4:
                        hidden_T(j, PAIRS - 1)
                    if t == 0 and part == 4:
                        pe.wait_ge(selg_ready, j + 1)
                        after(pe, hl_ready, j * PAIRS)
                        for b in range(NB):
                            last = transposed(bank[3][:, b * P:(b + 1) * P], selg[:, b, :], ident[:, :])
                        last.then_inc(selT_mm, 1)
                    if t == PAIRS - 1 and part == 3 and not extra:
                        gather(j + 1)
                if extra:
                    back(j)

            def back(j):
                pe.wait_ge(y_a, j + 1)
                pe.wait_ge(y_d, j + 1)
                pe.wait_ge(selT_ready, j + 1)
                for i in range(4):
                    after(pe, back_done, j * 8 + max(0, 2 * (i - 1)))
                    for a in range(2):
                        k = 2 * i + a
                        last = mm(bank[2 + i % 2][:, SEQ * a:SEQ * a + SEQ], y[:, k * P:(k + 1) * P], selT[:, :],
                                  start=True, stop=True)
                    last.then_inc(back_mm, 1)

            gather(0)
            job(0, 0)
            with pe.Fori(1, E) as e:
                job(e, e)
            back(E - 1)
            more_jobs(pe, job, extra=True)
            pe.wait_ge(x_final, 1)
            for i in range(4):
                if i >= 2:
                    pe.wait_ge(fin_evac, i - 1)
                for a in range(4):
                    last = transposed(bank[6 + i % 2][:, a * P:(a + 1) * P],
                                      xT[:, 4 * (i % 2) + a, (i // 2) * P:(i // 2 + 1) * P], ident[:, :])
                last.then_inc(fin_tp, 1)


NAMES = ["x", "c", "positions", "inv_freq", "ada_w", "ada_b", "mix_norm", "ffn_norm", "a_w_in", "a_conv_w", "a_conv_b",
         "a_gx_w", "a_gx_b", "a_ga_w", "a_ga_b", "a_lambda", "a_w_out", "kv_norm", "kv_ada_w", "kv_ada_b", "w_kv",
         "k_norm", "b_w_q", "b_q_norm", "b_sinks", "b_w_o", "f_w_gu", "f_w_down", "m_router", "m_w_gu", "m_w_down"]


def kernel(**inputs):
    import numpy as np
    import concourse.bacc as bacc
    from concourse.bass_utils import run_bass_kernel_spmd

    inv = (np.float32(10000.0) ** (-np.arange(0, HD, 2, dtype=np.float32) / np.float32(HD))).astype(np.float32)
    nc = bacc.Bacc("TRN2", target_bir_lowering=False, num_devices=1)
    arrays, args = {}, []
    for name in NAMES:
        a = np.ascontiguousarray(inv[None, :] if name == "inv_freq" else inputs[name])
        arrays[f"in_{name}"] = a
        args.append(nc.dram_tensor(f"in_{name}", a.shape, mybir.dt.from_np(a.dtype), kind="ExternalInput").ap())
    args.append(nc.dram_tensor("out_0", (1, SEQ, D), F32, kind="ExternalOutput").ap())
    build(nc, *args)
    r = run_bass_kernel_spmd(nc, [arrays], core_ids=[0])
    return r.results[0]["out_0"]
```
